# Optimizing a Trainium2 kernel written in Bass

```python
import math
import jax, jax.numpy as jnp
from jax import lax
import numpy as np

D_MODEL = 2048
BATCH = 1
SEQ = 256
DEPTH = 2

MEM_LEN = 256
N_MIXERS = 2
HEAD_DIM = 128
MIX_WIDTH = D_MODEL
CROSS_HEADS = 4
CROSS_WIDTH = CROSS_HEADS * HEAD_DIM
TOK_WIDTH = MIX_WIDTH - CROSS_WIDTH
CONV_WIDTH = 3
DIFF_HEAD_DIM = 64
DIFF_HEADS = TOK_WIDTH // (2 * DIFF_HEAD_DIM)
IN_WIDTH = 3 * TOK_WIDTH + CROSS_WIDTH + MIX_WIDTH
ROPE_THETA = 10000.0
RMS_EPS = 1e-6
Q_BLOCK = 128
NEG_BIG = -1e30
N_CONV_LAYERS = (DEPTH + 1) // 2
N_DIFF_LAYERS = DEPTH // 2

kernel_name = "hybrid_shortconv_diffattn_memxattn"

def _rms_norm(x, g):
    xf = x.astype(jnp.float32)
    xf = xf * lax.rsqrt(jnp.mean(xf * xf, axis=-1, keepdims=True) + RMS_EPS)
    return (xf * g.astype(jnp.float32)).astype(x.dtype)

def _rope(t, positions):
    d = t.shape[-1]
    inv_freq = ROPE_THETA ** (-jnp.arange(0, d, 2, dtype=jnp.float32) / d)
    ang = positions.astype(jnp.float32)[:, :, None] * inv_freq
    cos = jnp.cos(ang)[:, :, None, None, :]
    sin = jnp.sin(ang)[:, :, None, None, :]
    tf = t.astype(jnp.float32)
    t1, t2 = tf[..., : d // 2], tf[..., d // 2:]
    out = jnp.concatenate([t1 * cos - t2 * sin, t2 * cos + t1 * sin], axis=-1)
    return out.astype(t.dtype)

def _short_conv_mixer(proj_tok, conv_w):
    x_in, gate_b, gate_c = jnp.split(proj_tok, 3, axis=-1)
    u = gate_c * x_in
    s = u.shape[1]
    up = jnp.pad(u, ((0, 0), (CONV_WIDTH - 1, 0), (0, 0)))
    w = conv_w.astype(u.dtype)
    conv = sum(up[:, k:k + s, :] * w[:, k] for k in range(CONV_WIDTH))
    return gate_b * conv

def _diff_attention(q, k, v, lam):
    b, s, h, _, d = q.shape
    nb = s // Q_BLOCK
    scale = d ** -0.5
    qb = q.reshape(b, nb, Q_BLOCK, h, 2, d).transpose(1, 0, 2, 3, 4, 5)
    key_idx = jnp.arange(s)

    def block(args):
        q_blk, blk = args
        q_idx = blk * Q_BLOCK + jnp.arange(Q_BLOCK)
        scores = jnp.einsum('bqhmd,bkhmd->bhmqk', q_blk, k,
                            preferred_element_type=jnp.float32) * scale
        causal = key_idx[None, :] <= q_idx[:, None]
        scores = jnp.where(causal, scores, NEG_BIG)
        probs = jax.nn.softmax(scores, axis=-1)
        weights = probs[:, :, 0] - lam * probs[:, :, 1]
        return jnp.einsum('bhqk,bkhe->bqhe', weights.astype(v.dtype), v)

    out = lax.map(block, (qb, jnp.arange(nb)))
    return out.transpose(1, 0, 2, 3, 4).reshape(b, s, h, v.shape[-1])

def _diff_attention_mixer(proj_tok, positions, lam_params, subln_g, layer_idx):
    b, s, _ = proj_tok.shape
    q, k, v = jnp.split(proj_tok, 3, axis=-1)
    q = _rope(q.reshape(b, s, DIFF_HEADS, 2, DIFF_HEAD_DIM), positions)
    k = _rope(k.reshape(b, s, DIFF_HEADS, 2, DIFF_HEAD_DIM), positions)
    v = v.reshape(b, s, DIFF_HEADS, 2 * DIFF_HEAD_DIM)
    lambda_init = 0.8 - 0.6 * math.exp(-0.3 * layer_idx)
    lp = lam_params.astype(jnp.float32)
    lam = jnp.exp(jnp.sum(lp[0] * lp[1])) - jnp.exp(jnp.sum(lp[2] * lp[3])) + lambda_init
    o = _diff_attention(q, k, v, lam)
    o = _rms_norm(o, subln_g) * (1.0 - lambda_init)
    return o.reshape(b, s, TOK_WIDTH)

def _memory_cross_attention(q_mem, mem_n, w_kv):
    b, s, _ = q_mem.shape
    q = q_mem.reshape(b, s, CROSS_HEADS, HEAD_DIM)
    kv = mem_n @ w_kv
    km, vm = jnp.split(kv, 2, axis=-1)
    km = km.reshape(b, -1, CROSS_HEADS, HEAD_DIM)
    vm = vm.reshape(b, -1, CROSS_HEADS, HEAD_DIM)
    scores = jnp.einsum('bshd,bmhd->bhsm', q, km,
                        preferred_element_type=jnp.float32) * (HEAD_DIM ** -0.5)
    probs = jax.nn.softmax(scores, axis=-1)
    o = jnp.einsum('bhsm,bmhd->bshd', probs.astype(vm.dtype), vm)
    return o.reshape(b, s, CROSS_WIDTH)

def setup_inputs(seed: int = 0) -> dict:
    key = jax.random.key(seed)
    ks = jax.random.split(key, 14)
    f32 = jnp.float32
    x = jax.random.normal(ks[0], (BATCH, SEQ, D_MODEL), f32)
    mem = jax.random.normal(ks[1], (BATCH, MEM_LEN, D_MODEL), f32)
    offsets = jax.random.randint(ks[2], (BATCH, 1), 0, 1024, dtype=jnp.int32)
    positions = offsets + jnp.arange(SEQ, dtype=jnp.int32)[None, :]
    pre_norm = 1.0 + 0.05 * jax.random.normal(ks[3], (DEPTH, D_MODEL), f32)
    post_norm = 1.0 + 0.05 * jax.random.normal(ks[4], (DEPTH, D_MODEL), f32)
    mem_norm = 1.0 + 0.05 * jax.random.normal(ks[5], (DEPTH, D_MODEL), f32)
    w_in = jax.random.normal(ks[6], (DEPTH, D_MODEL, IN_WIDTH), f32) * D_MODEL ** -0.5
    w_kv_mem = jax.random.normal(ks[7], (DEPTH, D_MODEL, 2 * CROSS_WIDTH), f32) * D_MODEL ** -0.5
    w_out = jax.random.normal(ks[8], (DEPTH, MIX_WIDTH, D_MODEL), f32) * MIX_WIDTH ** -0.5
    conv_w = jax.random.normal(ks[9], (N_CONV_LAYERS, TOK_WIDTH, CONV_WIDTH), f32) * CONV_WIDTH ** -0.5
    diff_lambda = 0.1 * jax.random.normal(ks[10], (N_DIFF_LAYERS, 4, DIFF_HEAD_DIM), f32)
    diff_subln = 1.0 + 0.05 * jax.random.normal(ks[11], (N_DIFF_LAYERS, 2 * DIFF_HEAD_DIM), f32)
    return {"x": x, "mem": mem, "positions": positions, "pre_norm": pre_norm,
            "post_norm": post_norm, "mem_norm": mem_norm, "w_in": w_in,
            "w_kv_mem": w_kv_mem, "w_out": w_out, "conv_w": conv_w,
            "diff_lambda": diff_lambda, "diff_subln": diff_subln}

def reference(x, mem, positions, pre_norm, post_norm, mem_norm, w_in, w_kv_mem,
              w_out, conv_w, diff_lambda, diff_subln):
    for i in range(DEPTH):
        h = _rms_norm(x, pre_norm[i])
        proj = h @ w_in[i]
        proj_tok = proj[..., : 3 * TOK_WIDTH]
        q_mem = proj[..., 3 * TOK_WIDTH: 3 * TOK_WIDTH + CROSS_WIDTH]
        gate = proj[..., 3 * TOK_WIDTH + CROSS_WIDTH:]
        if i % N_MIXERS == 0:
            tok_out = _short_conv_mixer(proj_tok, conv_w[i // N_MIXERS])
        else:
            tok_out = _diff_attention_mixer(proj_tok, positions, diff_lambda[i // N_MIXERS],
                                            diff_subln[i // N_MIXERS], i)
        mem_n = _rms_norm(mem, mem_norm[i])
        cross_out = _memory_cross_attention(q_mem, mem_n, w_kv_mem[i])
        branch = jnp.concatenate([tok_out, cross_out], axis=-1) * jax.nn.silu(gate)
        y = branch @ w_out[i]
        x = x + _rms_norm(y, post_norm[i])
    return x


_drawn_inputs = setup_inputs


def setup_inputs(seed=0):
    import zlib

    import numpy as np

    out = dict(_drawn_inputs(seed))
    spreads = {}
    factors = {'mem_norm': 8.0, 'diff_lambda': 4.473, 'diff_subln': 8.0}
    for name, (base, spread) in spreads.items():
        noise = np.random.default_rng([zlib.crc32(name.encode()), seed]).standard_normal(out[name].shape)
        drawn = base * np.exp(spread * noise) if base else spread * noise
        out[name] = __import__('jax').numpy.asarray(drawn.astype(out[name].dtype))
    for name, factor in factors.items():
        out[name] = (out[name] * factor).astype(out[name].dtype)
    return out
```

```python
import math

import numpy as np
import concourse.bass as bass
from concourse import mybir

D_MODEL, SEQ, MEM_LEN, DEPTH = 2048, 256, 256, 2
HEAD_DIM, CROSS_HEADS, DIFF_DIM, CONV_WIDTH = 128, 4, 64, 3
CROSS_WIDTH = CROSS_HEADS * HEAD_DIM
TOK_WIDTH = D_MODEL - CROSS_WIDTH
ROPE_THETA, RMS_EPS, NEG_BIG = 10000.0, 1e-6, -1e30

P = 128
KT = D_MODEL // P
TT = SEQ // P
BCOLS = 256
ACOLS = 512
UNIT = 1024
SLOTS = 4
B_UNITS = KT * BCOLS // UNIT
A_UNITS = KT * ACOLS // UNIT
B_KT = KT // B_UNITS
A_KT = KT // A_UNITS
PAIRS = TOK_WIDTH // BCOLS
QM_COL = 3 * TOK_WIDTH
GATE_COL = QM_COL + CROSS_WIDTH
XGATE_COL = GATE_COL + TOK_WIDTH
OUT_ORDER = [0, 2, 4, 6, 8, 12, 14, 10]
LAMBDA_INIT = 0.8 - 0.6 * math.exp(-0.3 * 1)
TWO_PI = (6.28125, 2029 / 2 ** 20, 2 * math.pi - 6.28125 - 2029 / 2 ** 20)
ROUND = 1.5 * 2.0 ** 23
PI_BELOW = 3.1415925

G_KM0, U_KM0 = 0, 0
G_VM0, U_VM0 = 2, 8
G_QM0, U_QM0 = 3, 16
G_XG0, U_XG0 = 5, 24
G_MIX, U_MIX = 7, 32
G_OUT0, U_OUT0 = 31, 128
G_KM1, U_KM1 = 35, 160
G_VM1, U_VM1 = 37, 168
G_QM1, U_QM1 = 38, 176
G_V, U_V = 40, 184
G_PAIR, U_PAIR = 43, 208
G_XG1, U_XG1 = 61, 280
G_OUT1, U_OUT1 = 63, 288
UNITS = U_OUT1 + 4 * A_UNITS

STEPS = KT // 2
N_MEM0, N_X, N_MEM1, N_H1 = 0, STEPS, 2 * STEPS, 3 * STEPS


def columns_before(G, row_groups):
    return G - row_groups


class Steps:

    def __init__(self, eng, sem, base=0):
        self.eng, self.sem, self.base, self.n = eng, sem, base, 0

    def did(self, ins):
        ins.then_inc(self.sem, 1)
        self.n += 1

    def need(self):
        if isinstance(self.base, int) and self.base + self.n == 0:
            return
        self.eng.wait_ge(self.sem, self.base + self.n)


def build(nc, x_in, mem_in, positions, pre_norm, post_norm, mem_norm, w_in, w_kv_mem, w_out,
          conv_w, diff_lambda, diff_subln, rope_consts, out):
    f32, f32r, i32 = mybir.dt.float32, mybir.dt.float32r, mybir.dt.int32
    ALU, ACT, AX = mybir.AluOpType, mybir.ActivationFunctionType, mybir.AxisListType.X

    def sb(name, shape, dt=f32):
        return nc.alloc_sbuf_tensor(name, shape, dt).ap()

    XA = sb("hT_split", [P, KT, 2 * SEQ], f32r)
    XC = sb("branchT_split", [P, KT, 2 * SEQ], f32r)
    xb_at = -(-nc.sbuf_base // 32) * 32
    XB = sb("memT_split", [P, KT, 2 * MEM_LEN], f32r)
    L1 = nc.alloc_sbuf_tensor_at("layer1_area", [P, KT * 2 * MEM_LEN], f32, offset=xb_at).ap()
    xres = sb("x_residual", [P, TT, D_MODEL])
    S = sb("stage_area", [P, 2 * D_MODEL])
    raw = sb("raw_ring", [P, SLOTS, UNIT])
    whi = sb("hi_ring", [P, SLOTS, UNIT], f32r)
    wlo = sb("lo_ring", [P, SLOTS, UNIT], f32r)
    kmT = sb("kmT", [P, CROSS_HEADS, MEM_LEN])
    vm = sb("vm", [P, MEM_LEN // P, CROSS_WIDTH])
    qmT = sb("qmT", [P, CROSS_HEADS, SEQ])
    area = sb("layer0_area", [P, D_MODEL + 4])
    small = sb("small_terms", [P, 2, 256])
    xgate = sb("cross_gate0", [P, CROSS_HEADS, SEQ])
    ident = sb("ident", [P, P])
    mask = sb("causal_mask", [P, P])
    cosT = sb("cosT", [P, SEQ])
    sinT = sb("sinT", [P, SEQ])
    mem_rstd_row = sb("mem_rstd_row", [P, MEM_LEN])
    gT = sb("normT", [P, 2 * DEPTH * KT])
    convw = sb("convw", [P, 2 * PAIRS * CONV_WIDTH])
    cols = sb("columns", [P, 96])

    mem_raw = S.rearrange("p (t d) -> p t d", t=TT)
    y_all = S.rearrange("p (t d) -> p t d", t=TT)
    V = S[:, 0:TT * TOK_WIDTH].rearrange("p (t d) -> p t d", t=TT)
    tanh1 = S[:, 3072:3584].rearrange("p (c t) -> p c t", c=2)
    br1 = S[:, 3584:4096].rearrange("p (c t) -> p c t", c=2)
    xprob = [a[:, 0:2048].rearrange("p (h k) -> p h k", h=2 * CROSS_HEADS) for a in (S, L1)]
    xprobT = [a[:, 2048:4096].rearrange("p (h k) -> p h k", h=CROSS_HEADS) for a in (S, L1)]
    crossT1 = L1[:, 7168:8192].rearrange("p (h t) -> p h t", h=CROSS_HEADS)

    def l1(at):
        return L1[:, at:at + 512]
    qT, qrot, kT, krot = l1(0), l1(512), l1(1024), l1(1536)
    sgate = [l1(2048).rearrange("p (c t) -> p c t", c=2), l1(2560).rearrange("p (c t) -> p c t", c=2)]
    prob = L1[:, 3072:4608].rearrange("p (h m k) -> p h m k", h=2, m=2)
    probT = L1[:, 4608:5376].rearrange("p (h k) -> p h k", h=2)
    o_sb = l1(5376).rearrange("p (g e) -> p g e", g=4)
    o_sq = l1(5888).rearrange("p (g e) -> p g e", g=4)
    val1 = l1(6400).rearrange("p (c t) -> p c t", c=2)
    gpost = area[:, 0:D_MODEL]
    xin = area[:, 0:512].rearrange("p (c t) -> p c t", c=2)
    val0 = area[:, 512:1024].rearrange("p (c t) -> p c t", c=2)
    conv = area[:, 1024:1536].rearrange("p (c t) -> p c t", c=2)
    upad = area[:, 1536:2052].rearrange("p (c t) -> p c t", c=2)
    xg_flat = xgate.rearrange("p h t -> p (h t)")
    norm_rows, pos_i = xg_flat[0:64, 0:128], xg_flat[:, 128:384].bitcast(i32)
    lam_in, diag, ones = xg_flat[:, 384:640], xg_flat[:, 640:896], xg_flat[:, 896:1024]
    y_junk = xg_flat[:, 0:512]
    inv_freq, rope_sign, subg = cols[:, 0:1], cols[:, 1:2], cols[:, 2:3]
    mem_rstd, x_rstd, y_rstd = cols[:, 4:6], cols[:, 6:8], cols[:, 8:10]
    lam_dot, lam_exp, neg_lam = cols[:, 10:12], cols[:, 12:14], cols[:, 14:15]
    ss = cols[:, 16:24]
    y_ss = cols[:, 24:32]
    rs_v, rs_t, rs_i = cols[:, 32:36], cols[:, 36:40], cols[:, 40:44]
    xmax, xnegmax, xsum, xrcp = (cols[:, 44 + 8 * i:52 + 8 * i] for i in range(4))
    o_rstd = cols[:, 76:80]
    subg_raw = cols[:, 80:81]

    ps = nc.alloc_psum_tensor("psum", [P, 8, 512], f32).ap()

    def banks(s):
        return ps[:, 2 * s:2 * s + 2, :]

    score = ps[:, 4:8, :].rearrange("p (m b) c -> p m b c", b=2)
    score1 = score[:, :, 0, :].rearrange("p m (h k) -> p m h k", h=2)
    score0 = score[:, :, 1, 0:256].rearrange("p m (h k) -> p m h k", h=2)

    def sem(name):
        return nc.alloc_semaphore(name)

    raw_loaded = [sem(f"raw_loaded{i}") for i in range(SLOTS)]
    hi_ready, lo_ready = sem("hi_ready"), sem("lo_ready")
    unit_done = sem("unit_done")
    small_copied = sem("small_copied")
    bank_free = sem("bank_free")
    mem_loaded = [sem(f"mem_loaded{i}") for i in range(4)]
    x_loaded, rows_loaded, misc_loaded = sem("x_loaded"), sem("rows_loaded"), sem("misc_loaded")
    gpost_loaded, rot_loaded, out_stored = sem("gpost_loaded"), sem("rot_loaded"), sem("out_stored")
    ident_step, const_ready = sem("ident_step"), sem("const_ready")
    tr_done, tr_hi, tr_lo = sem("tr_done"), sem("tr_hi"), sem("tr_lo")
    norm_turned, norm_ready = sem("norm_turned"), sem("norm_ready")
    diag_ready, row_done, row_copied = sem("diag_ready"), sem("row_done"), sem("row_copied")
    x_stat, xs_ready = sem("x_stat"), sem("xs_ready")
    angle_ready, table_ready = sem("angle_ready"), sem("table_ready")
    km_ready = sem("km_ready")
    xs_done, xmax_ready, xexp_done, xprob_ready = (sem("xscore_done"), sem("xmax_ready"),
                                                   sem("xexp_done"), sem("xprob_ready"))
    xt_done, xpt_ready, xo_done, xo_taken = sem("xturn_done"), sem("xprobT_ready"), sem("xout_done"), sem("xout_taken")
    tanh_done, branch_ready = sem("tanh_done"), sem("branch_ready")
    rope_done, s_done, max_ready, exp_done = sem("rope_done"), sem("score_done"), sem("max_ready"), sem("exp_done")
    w_ready, wt_done, wt_ready = sem("weights_ready"), sem("weights_turned"), sem("weightsT_ready")
    pv_done, o_copied, on_ready, n_done = sem("pv_done"), sem("o_copied"), sem("o_normed"), sem("o_turned")
    out_ready = sem("out_ready")
    dve_step = sem("dve_step")

    X_SCALE, D_SCALE = HEAD_DIM ** -0.5, DIFF_DIM ** -0.5
    block_cm = nc.Block()
    block = block_cm.__enter__()

    @block.sync
    def _(sp):
        def unit(u, slot, dst, src):
            if not isinstance(u, int) or u >= SLOTS:
                sp.wait_ge(lo_ready, u - SLOTS + 1)
            sp.dma_start(dst, src).then_inc(raw_loaded[slot], 16)

        def column_group(u, w, col):
            w = w.rearrange("(k p) n -> p k n", p=P)
            for n in range(B_UNITS):
                unit(u + n, n % SLOTS, raw[:, n % SLOTS, :].rearrange("p (k c) -> p k c", k=B_KT),
                     w[:, B_KT * n:B_KT * (n + 1), bass.ds(col, BCOLS)])

        def row_group(u, w, col, order):
            w = w.rearrange("(k p) n -> p k n", p=P)
            for n, k in enumerate(order):
                unit(u + n, n % SLOTS, raw[:, n % SLOTS, :].rearrange("p (k c) -> p k c", k=A_KT),
                     w[:, k:k + A_KT, col:col + ACOLS])

        in_order = list(range(0, KT, A_KT))

        def memory(l, u):
            for i in range(2):
                column_group(u + B_UNITS * i, w_kv_mem[l], BCOLS * i)
            row_group(u + 2 * B_UNITS, w_kv_mem[l], CROSS_WIDTH, in_order)

        memory(0, U_KM0)
        for i in range(2):
            column_group(U_QM0 + B_UNITS * i, w_in[0], QM_COL + BCOLS * i)
        for i in range(2):
            column_group(U_XG0 + B_UNITS * i, w_in[0], XGATE_COL + BCOLS * i)
        with sp.Fori(0, PAIRS) as j:
            for g, col in enumerate((0, 2 * TOK_WIDTH, TOK_WIDTH, GATE_COL)):
                column_group(j * (4 * B_UNITS) + (U_MIX + B_UNITS * g), w_in[0], j * BCOLS + col)
        for g in range(4):
            row_group(U_OUT0 + A_UNITS * g, w_out[0], ACOLS * g, OUT_ORDER)
        memory(1, U_KM1)
        for i in range(2):
            column_group(U_QM1 + B_UNITS * i, w_in[1], QM_COL + BCOLS * i)
        for g in range(3):
            row_group(U_V + A_UNITS * g, w_in[1], 2 * TOK_WIDTH + ACOLS * g, in_order)
        with sp.Fori(0, PAIRS) as p:
            for g, col in enumerate((0, TOK_WIDTH, GATE_COL)):
                column_group(p * (3 * B_UNITS) + (U_PAIR + B_UNITS * g), w_in[1], p * BCOLS + col)
        for i in range(2):
            column_group(U_XG1 + B_UNITS * i, w_in[1], XGATE_COL + BCOLS * i)
        for g in range(4):
            row_group(U_OUT1 + A_UNITS * g, w_out[1], ACOLS * g, OUT_ORDER)
        for t in range(TT):
            for h in range(2):
                sp.wait_ge(out_ready, 2 * t + h + 1)
                sp.dma_start(out[0, P * t:P * (t + 1), 1024 * h:1024 * (h + 1)],
                             xres[:, t, 1024 * h:1024 * (h + 1)]).then_inc(out_stored, 16)
        sp.wait_ge(out_stored, 16 * 2 * TT)

    @block.gpsimd
    def _(pool):
        nc.gpsimd.memset(ident, 0.0).then_inc(ident_step, 1)
        nc.gpsimd.memset(mask, 0.0).then_inc(ident_step, 1)
        nc.gpsimd.memset(ones, 1.0).then_inc(const_ready, 1)
        pool.wait_ge(ident_step, 2)
        nc.gpsimd.affine_select(out=ident, in_=ident, compare_op=ALU.not_equal, fill=1.0, base=0,
                                pattern=[[-1, P]], channel_multiplier=1).then_inc(const_ready, 1)
        nc.gpsimd.affine_select(out=mask, in_=mask, compare_op=ALU.is_ge, fill=NEG_BIG, base=0,
                                pattern=[[-1, P]], channel_multiplier=1).then_inc(const_ready, 1)

    @block.tensor
    def _(pe):
        mm = nc.tensor.matmul

        def first_bank_wait(G):
            if not isinstance(G, int) or G >= 2:
                pe.wait_ge(bank_free, G - 1)

        def column_group(G, u, s, X, x_steps=None, mid=None):
            first_bank_wait(G)
            for n in range(B_UNITS):
                if mid and n == B_UNITS // 2:
                    mid()
                if x_steps is not None:
                    pe.wait_ge(tr_lo, x_steps + 2 * (n + 1))
                pe.wait_ge(lo_ready, u + n + 1)
                hi = whi[:, n % SLOTS, :].rearrange("p (k c) -> p k c", k=B_KT)
                lo = wlo[:, n % SLOTS, :].rearrange("p (k c) -> p k c", k=B_KT)
                for k in range(B_KT):
                    kt = B_KT * n + k
                    for c in range(2):
                        o = banks(s)[:, c, :]
                        mm(o, hi[:, k, P * c:P * (c + 1)], X[:, kt, :], start=kt == 0, stop=False)
                        last = mm(o[:, SEQ:], lo[:, k, P * c:P * (c + 1)], X[:, kt, 0:SEQ],
                                  start=False, stop=kt == KT - 1)
                last.then_inc(unit_done, 1)

        def row_group(G, u, s, X, order, before=None, mid=None, mid_at=4):
            first_bank_wait(G)
            for n, k0 in enumerate(order):
                if mid and n == mid_at:
                    mid()
                if before:
                    before(n)
                pe.wait_ge(lo_ready, u + n + 1)
                hi = whi[:, n % SLOTS, :].rearrange("p (k c) -> p k c", k=A_KT)
                lo = wlo[:, n % SLOTS, :].rearrange("p (k c) -> p k c", k=A_KT)
                for k in range(A_KT):
                    for t in range(TT):
                        xh = X[:, k0 + k, P * t:P * (t + 1)]
                        xl = X[:, k0 + k, SEQ + P * t:SEQ + P * (t + 1)]
                        o = banks(s)[:, t, :]
                        first, final = n == 0 and k == 0, n == len(order) - 1 and k == A_KT - 1
                        mm(o, xl, hi[:, k, :], start=first, stop=False)
                        mm(o, xh, lo[:, k, :], start=False, stop=False)
                        last = mm(o, xh, hi[:, k, :], start=False, stop=final)
                last.then_inc(unit_done, 1)

        def turn(n, src, ready=None):
            if n >= 4:
                pe.wait_ge(tr_lo, n - 3)
            if ready:
                ready()
            for k in range(2):
                kt = 2 * (n % STEPS) + k
                for t in range(TT):
                    last = nc.tensor.transpose(ps[:, 4 + n % 4, 256 * k + P * t:256 * k + P * (t + 1)],
                                               src[:, t, P * kt:P * (kt + 1)], ident)
            last.then_inc(tr_done, 1)

        def cross_scores(l):
            pe.wait_ge(km_ready, 2 * (l + 1))
            for h in range(CROSS_HEADS):
                for t in range(TT):
                    last = mm(ps[:, 4 + h, 256 * t:256 * (t + 1)], qmT[:, h, P * t:P * (t + 1)],
                              kmT[:, h, :], start=True, stop=True)
            last.then_inc(xs_done, 1)

        def cross_turn(l):
            pe.wait_ge(xprob_ready, l + 1)
            for h in range(CROSS_HEADS):
                for m in range(MEM_LEN // P):
                    for t in range(TT):
                        last = nc.tensor.transpose(ps[:, 4 + h, 256 * m + P * t:256 * m + P * (t + 1)],
                                                   xprob[l][:, 2 * h + t, P * m:P * (m + 1)], ident)
                last.then_inc(xt_done, 1)

        def cross_values(l):
            pe.wait_ge(xpt_ready, 4 * (l + 1))
            for h in range(CROSS_HEADS):
                for m in range(MEM_LEN // P):
                    last = mm(ps[:, 4 + h // 2, 256 * (h % 2):256 * (h % 2) + 256],
                              vm[:, m, P * h:P * (h + 1)], xprobT[l][:, h, 256 * m:256 * (m + 1)],
                              start=m == 0, stop=m == 1)
            last.then_inc(xo_done, 1)

        in_order = list(range(0, KT, A_KT))

        pe.wait_ge(const_ready, 3)
        pe.wait_ge(rows_loaded, 32)
        nc.tensor.transpose(ps[:, 7, 0:64], norm_rows, ident[0:64, 0:64]).then_inc(norm_turned, 1)
        for n in range(STEPS):
            def ready(n=n):
                if n % 2 == 0:
                    pe.wait_ge(mem_loaded[n // 2], 16)
                if n == 3:
                    pe.wait_ge(norm_ready, 1)
            turn(N_MEM0 + n, mem_raw, ready)
        column_group(G_KM0, U_KM0, 0, XB, x_steps=N_MEM0)
        pe.wait_ge(diag_ready, 2)
        pe.wait_ge(tr_lo, STEPS)
        for t in range(TT):
            last = mm(ps[:, 7, P * t:P * (t + 1)], ones, diag[:, P * t:P * (t + 1)], start=True, stop=True)
        last.then_inc(row_done, 1)
        column_group(G_KM0 + 1, U_KM0 + B_UNITS, 1, XB)
        pe.wait_ge(xs_ready, 2)
        pe.wait_ge(row_copied, 1)
        for n in range(4):
            turn(N_X + n, xres)
        row_group(G_VM0, U_VM0, 0, XB, in_order, mid=lambda: [turn(N_X + n, xres) for n in range(4, 8)])
        column_group(G_QM0, U_QM0, 1, XA, x_steps=N_X)
        for n in range(4):
            turn(N_MEM1 + n, mem_raw)
        column_group(G_QM0 + 1, U_QM0 + B_UNITS, 0, XA)
        for n in range(4, 8):
            turn(N_MEM1 + n, mem_raw)
        column_group(G_XG0, U_XG0, 1, XA)
        pe.wait_ge(bank_free, G_QM0 + 2)
        pe.wait_ge(tr_lo, N_MEM1 + STEPS)
        cross_scores(0)
        column_group(G_XG0 + 1, U_XG0 + B_UNITS, 0, XA)
        cross_turn(0)
        with pe.Fori(0, PAIRS) as j:
            for g in range(4):
                column_group(j * 4 + (G_MIX + g), j * (4 * B_UNITS) + (U_MIX + B_UNITS * g),
                             (G_MIX + g) % 2, XA)
        pe.wait_ge(bank_free, G_VM0 + 1)
        cross_values(0)

        def branch_wait(counts):
            def before(n):
                if n in counts:
                    pe.wait_ge(branch_ready, counts[n])
            return before

        for g in range(4):
            row_group(G_OUT0 + g, U_OUT0 + A_UNITS * g, (G_OUT0 + g) % 2, XC, OUT_ORDER,
                      before=branch_wait({0: PAIRS - 1, 5: PAIRS + 1}))
        column_group(G_KM1, U_KM1, G_KM1 % 2, XB, x_steps=N_MEM1)
        column_group(G_KM1 + 1, U_KM1 + B_UNITS, (G_KM1 + 1) % 2, XB)
        pe.wait_ge(xs_ready, 4)
        pe.wait_ge(xo_taken, 1)
        for n in range(4):
            turn(N_H1 + n, y_all)
        row_group(G_VM1, U_VM1, G_VM1 % 2, XB, in_order,
                  mid=lambda: [turn(N_H1 + n, y_all) for n in range(4, 8)])
        column_group(G_QM1, U_QM1, G_QM1 % 2, XA, x_steps=N_H1)
        column_group(G_QM1 + 1, U_QM1 + B_UNITS, (G_QM1 + 1) % 2, XA)
        for g in range(3):
            row_group(G_V + g, U_V + A_UNITS * g, (G_V + g) % 2, XA, in_order)
            if g == 0:
                pe.wait_ge(bank_free, G_QM1 + 2)
                cross_scores(1)
            elif g == 1:
                cross_turn(1)
            else:
                cross_values(1)

        def diff_turn(p):
            pe.wait_ge(w_ready, p + 1)
            for h in range(2):
                for b in range(3):
                    last = nc.tensor.transpose(ps[:, 4 + h, P * b:P * (b + 1)],
                                               prob[:, h, 0, P * b:P * (b + 1)], ident)
            last.then_inc(wt_done, 1)

        def diff_values(p):
            pe.wait_ge(wt_ready, p + 1)
            for h in range(2):
                o = ps[:, 6, 256 * h:256 * (h + 1)]
                v = [V[:, t, bass.ds(p * (2 * P) + P * h, P)] for t in range(TT)]
                mm(o[:, 0:P], probT[:, h, 0:P], v[0], start=True, stop=True)
                mm(o[:, P:], probT[:, h, P:2 * P], v[0], start=True, stop=False)
                last = mm(o[:, P:], probT[:, h, 2 * P:], v[1], start=False, stop=True)
            last.then_inc(pv_done, 1)

        def diff_out_turn(p):
            pe.wait_ge(on_ready, p + 1)
            for g in range(4):
                last = nc.tensor.transpose(ps[:, 7, P * g:P * (g + 1)], o_sb[:, g, :], ident)
            last.then_inc(n_done, 1)

        def diff_scores(p, after):
            pe.wait_ge(rope_done, p * 2 + 2)
            if after is not None:
                pe.wait_ge(branch_ready, after)
            for m in range(2):
                for h in range(2):
                    rows = slice(DIFF_DIM * m, DIFF_DIM * (m + 1))
                    for t in range(TT):
                        o = (score0 if t == 0 else score1)[:, m, h, :]
                        last = mm(o, qT[rows, 256 * h + P * t:256 * h + P * (t + 1)],
                                  kT[rows, 256 * h:256 * h + P * (t + 1)], start=True, stop=True)
            last.then_inc(s_done, 1)

        def pair(p, s, first=False):
            G, u = p * 3 + G_PAIR, p * (3 * B_UNITS) + U_PAIR
            column_group(G, u, s, XA)
            if not first:
                diff_turn(p - 1)
            column_group(G + 1, u + B_UNITS, 1 - s, XA, mid=None if first else lambda: diff_values(p - 1))
            column_group(G + 2, u + 2 * B_UNITS, s, XA, mid=None if first else lambda: diff_out_turn(p - 1))
            diff_scores(p, None if first else p + (PAIRS + 1))

        pe.wait_ge(xo_taken, 2)
        pair(0, G_PAIR % 2, first=True)
        with pe.Fori(1, PAIRS - 1, 2) as p:
            pair(p, (G_PAIR + 1) % 2)
            pair(p + 1, G_PAIR % 2)
        pair(PAIRS - 1, (G_PAIR + 1) % 2)
        column_group(G_XG1, U_XG1, G_XG1 % 2, XA)
        diff_turn(PAIRS - 1)
        column_group(G_XG1 + 1, U_XG1 + B_UNITS, (G_XG1 + 1) % 2, XA,
                     mid=lambda: diff_values(PAIRS - 1))
        done0 = PAIRS + 1
        for g in range(4):
            row_group(G_OUT1 + g, U_OUT1 + A_UNITS * g, (G_OUT1 + g) % 2, XC, OUT_ORDER,
                      before=branch_wait({0: done0 + PAIRS - 1, 5: done0 + PAIRS, 6: done0 + PAIRS + 1,
                                          7: done0 + PAIRS + 2}),
                      mid=(lambda: diff_out_turn(PAIRS - 1)) if g == 0 else None, mid_at=2)

    @block.scalar
    def _(act):
        run = nc.scalar.activation
        act.dma_start(norm_rows[0:32, :], pre_norm.rearrange("l (k p) -> (l k) p", p=P)).then_inc(rows_loaded, 16)
        act.dma_start(norm_rows[32:64, :], mem_norm.rearrange("l (k p) -> (l k) p", p=P)).then_inc(rows_loaded, 16)
        mem_v = mem_in[0].rearrange("(t p) d -> p t d", p=P)
        for i in range(4):
            act.dma_start(mem_raw[:, :, 512 * i:512 * (i + 1)], mem_v[:, :, 512 * i:512 * (i + 1)])\
               .then_inc(mem_loaded[i], 16)
        x_v = x_in[0].rearrange("(t p) d -> p t d", p=P)
        act.dma_start(xres, x_v).then_inc(x_loaded, 16)
        act.dma_start(cols[:, 0:2], rope_consts).then_inc(misc_loaded, 16)
        act.dma_start(subg_raw, diff_subln[0].rearrange("(p a) -> p a", a=1)).then_inc(misc_loaded, 16)
        act.dma_start(pos_i, positions[0:1, :].partition_broadcast(P)[:, 0, :]).then_inc(misc_loaded, 16)
        act.dma_start(lam_in, diff_lambda.rearrange("l a d -> l (a d)").partition_broadcast(P)[:, 0, :])\
           .then_inc(misc_loaded, 16)
        act.dma_start(convw.rearrange("p (t k) -> p t k", k=CONV_WIDTH),
                      conv_w[0].rearrange("(t p) k -> p t k", p=P)).then_inc(misc_loaded, 16)

        def high(u, n, n0=0):
            for i in range(n0, n):
                slot = i % SLOTS
                act.wait_ge(raw_loaded[slot], (u + (i - slot)) * (16 // SLOTS) + 16)
                if not isinstance(u, int) or u + i >= SLOTS:
                    act.wait_ge(unit_done, u + (i - SLOTS + 1))
                run(whi[:, slot, :], raw[:, slot, :], ACT.Copy).then_inc(hi_ready, 1)

        def take_small(G, u, s):
            act.wait_ge(unit_done, u + B_UNITS)
            if not isinstance(G, int) or G >= 1:
                act.wait_ge(bank_free, G)
            run(small, banks(s)[:, :, SEQ:], ACT.Copy).then_inc(small_copied, 1)

        def column_group(G, u, s, mid=None):
            high(u + SLOTS, B_UNITS // 2)
            if mid:
                mid()
            high(u + SLOTS, B_UNITS, B_UNITS // 2)
            take_small(G, u, s)

        def row_group(G, u, s, outs, scale=None, mid=None, mid_at=4):
            n = min(A_UNITS, UNITS - (u + SLOTS))
            high(u + SLOTS, mid_at)
            if mid:
                mid()
            high(u + SLOTS, n, mid_at)
            act.wait_ge(unit_done, u + A_UNITS)
            act.wait_ge(bank_free, G)
            if scale is None:
                run(outs, banks(s), ACT.Copy).then_inc(bank_free, 1)
            else:
                run(outs[:, 0, :], banks(s)[:, 0, :], ACT.Copy, scale=scale[:, 0:1])
                run(outs[:, 1, :], banks(s)[:, 1, :], ACT.Copy, scale=scale[:, 1:2]).then_inc(bank_free, 1)

        def turned(n, X, g0):
            act.wait_ge(tr_done, n + 1)
            for k in range(2):
                kt = 2 * (n % STEPS) + k
                last = run(X[:, kt, 0:256], ps[:, 4 + n % 4, 256 * k:256 * (k + 1)], ACT.Copy,
                           scale=gT[:, g0 + kt:g0 + kt + 1])
            last.then_inc(tr_hi, 1)

        def cross_exp(l):
            act.wait_ge(xmax_ready, l + 1)
            for g in range(2 * CROSS_HEADS):
                run(xprob[l][:, g, :], ps[:, 4 + g // 2, 256 * (g % 2):256 * (g % 2) + 256], ACT.Exp,
                    bias=xnegmax[:, g:g + 1], scale=X_SCALE, accum_out=xsum[:, g:g + 1]).then_inc(xexp_done, 1)

        def cross_take(l):
            for h in range(CROSS_HEADS):
                act.wait_ge(xt_done, 4 * l + h + 1)
                run(xprobT[l][:, h, :], ps[:, 4 + h, :], ACT.Copy).then_inc(xpt_ready, 1)

        act.wait_ge(norm_ready, 1)
        for n in range(STEPS):
            turned(N_MEM0 + n, XB, 2 * KT)
            if n < SLOTS:
                high(0, n + 1, n)
        column_group(G_KM0, U_KM0, 0)
        column_group(G_KM0 + 1, U_KM0 + B_UNITS, 1)
        act.wait_ge(x_stat, 1)
        for t in range(TT):
            run(xres[:, t, :], xres[:, t, :], ACT.Copy, scale=x_rstd[:, t:t + 1]).then_inc(xs_ready, 1)
        for n in range(4):
            turned(N_X + n, XA, 0)
        row_group(G_VM0, U_VM0, 0, vm, scale=mem_rstd,
                  mid=lambda: [turned(N_X + n, XA, 0) for n in range(4, 8)])
        act.wait_ge(angle_ready, 1)
        run(cosT, cosT, ACT.Sin)
        run(sinT, sinT, ACT.Sin)
        run(lam_exp, lam_dot, ACT.Exp).then_inc(table_ready, 1)
        act.wait_ge(tr_lo, N_X + STEPS)
        act.dma_start(xres, x_v).then_inc(x_loaded, 16)
        column_group(G_QM0, U_QM0, 1)
        for n in range(4):
            turned(N_MEM1 + n, XB, 3 * KT)
        column_group(G_QM0 + 1, U_QM0 + B_UNITS, 0)
        for n in range(4, 8):
            turned(N_MEM1 + n, XB, 3 * KT)

        def tanh_of(G, src, dst):
            act.wait_ge(bank_free, G + 1)
            run(dst, src, ACT.Tanh, scale=0.5).then_inc(tanh_done, 1)

        column_group(G_XG0, U_XG0, 1)
        tanh_of(G_XG0, val0, xin)
        cross_exp(0)
        column_group(G_XG0 + 1, U_XG0 + B_UNITS, 0)
        tanh_of(G_XG0 + 1, val0, xin)
        cross_take(0)
        with act.Fori(0, PAIRS) as j:
            for g in range(4):
                G = j * 4 + (G_MIX + g)
                column_group(G, j * (4 * B_UNITS) + (U_MIX + B_UNITS * g), (G_MIX + g) % 2)
            tanh_of(G, val0, xin)
        act.wait_ge(branch_ready, PAIRS + 1)
        act.dma_start(gpost, post_norm[0:1, :].partition_broadcast(P)[:, 0, :]).then_inc(gpost_loaded, 16)
        for g in range(4):
            row_group(G_OUT0 + g, U_OUT0 + A_UNITS * g, (G_OUT0 + g) % 2, y_all[:, :, ACOLS * g:ACOLS * (g + 1)])
        column_group(G_KM1, U_KM1, G_KM1 % 2)
        column_group(G_KM1 + 1, U_KM1 + B_UNITS, (G_KM1 + 1) % 2)
        act.wait_ge(x_stat, 2)
        act.dma_start(gpost, post_norm[1:2, :].partition_broadcast(P)[:, 0, :]).then_inc(gpost_loaded, 16)
        for t in range(TT):
            run(y_all[:, t, :], xres[:, t, :], ACT.Copy, scale=x_rstd[:, t:t + 1]).then_inc(xs_ready, 1)
        for n in range(4):
            turned(N_H1 + n, XA, KT)
        row_group(G_VM1, U_VM1, G_VM1 % 2, vm, scale=mem_rstd,
                  mid=lambda: [turned(N_H1 + n, XA, KT) for n in range(4, 8)])
        column_group(G_QM1, U_QM1, G_QM1 % 2)
        column_group(G_QM1 + 1, U_QM1 + B_UNITS, (G_QM1 + 1) % 2)
        for g in range(3):
            row_group(G_V + g, U_V + A_UNITS * g, (G_V + g) % 2, V[:, :, ACOLS * g:ACOLS * (g + 1)])
            if g == 0:
                cross_exp(1)
            elif g == 1:
                cross_take(1)

        def swap_halves(G, src, dst):
            act.wait_ge(bank_free, G + 1)
            for b in range(4):
                o = 32 * (b ^ 1)
                act.dma_start(dst[32 * b:32 * b + 32, :], src[o:o + 32, :]).then_inc(rot_loaded, 16)

        def take_weights(p):
            act.wait_ge(wt_done, p + 1)
            run(probT, ps[:, 4:6, 0:3 * P], ACT.Copy).then_inc(wt_ready, 1)

        def take_values(p):
            act.wait_ge(pv_done, p + 1)
            run(o_sb, ps[:, 6, :].rearrange("p (g e) -> p g e", g=4), ACT.Copy).then_inc(o_copied, 1)

        def exps(p):
            act.wait_ge(max_ready, p + 1)
            for m in range(2):
                for h in range(2):
                    for t in range(TT):
                        i = 4 * m + 2 * h + t
                        run(prob[:, h, m, P * t:P * (1 + 2 * t)], (score0 if t == 0 else score1)[:, m, h, :],
                            ACT.Exp, bias=xnegmax[:, i:i + 1], scale=D_SCALE,
                            accum_out=xsum[:, i:i + 1]).then_inc(exp_done, 1)

        def pair(p, s, first=False):
            G, u = p * 3 + G_PAIR, p * (3 * B_UNITS) + U_PAIR
            column_group(G, u, s)
            swap_halves(G, qT, qrot)
            if not first:
                take_weights(p - 1)
            column_group(G + 1, u + B_UNITS, 1 - s, mid=None if first else lambda: take_values(p - 1))
            swap_halves(G + 1, kT, krot)
            column_group(G + 2, u + 2 * B_UNITS, s)
            tanh_of(G + 2, val1, tanh1)
            exps(p)

        pair(0, G_PAIR % 2, first=True)
        with act.Fori(1, PAIRS - 1, 2) as p:
            pair(p, (G_PAIR + 1) % 2)
            pair(p + 1, G_PAIR % 2)
        pair(PAIRS - 1, (G_PAIR + 1) % 2)
        column_group(G_XG1, U_XG1, G_XG1 % 2)
        tanh_of(G_XG1, val1, tanh1)
        take_weights(PAIRS - 1)
        column_group(G_XG1 + 1, U_XG1 + B_UNITS, (G_XG1 + 1) % 2, mid=lambda: take_values(PAIRS - 1))
        tanh_of(G_XG1 + 1, val1, tanh1)
        for g in range(4):
            row_group(G_OUT1 + g, U_OUT1 + A_UNITS * g, (G_OUT1 + g) % 2, y_all[:, :, ACOLS * g:ACOLS * (g + 1)],
                      mid_at=2)

    @block.vector
    def _(dve):
        V_ = nc.vector
        MULT, ADD, SUB, MAX, MIN = ALU.mult, ALU.add, ALU.subtract, ALU.max, ALU.min

        def low(u, n, n0=0):
            for i in range(n0, n):
                slot = i % SLOTS
                dve.wait_ge(hi_ready, u + (i + 1))
                V_.tensor_tensor(wlo[:, slot, :], raw[:, slot, :], whi[:, slot, :].bitcast(f32), SUB)\
                  .then_inc(lo_ready, 1)

        def combine(G, columns, u, s, dst):
            dve.wait_ge(lo_ready, u + (SLOTS + B_UNITS))
            dve.wait_ge(small_copied, columns + 1)
            V_.tensor_tensor(dst, banks(s)[:, :, 0:SEQ], small, ADD).then_inc(bank_free, 1)

        def column_group(G, columns, u, s, dst, mid=None):
            low(u + SLOTS, B_UNITS // 2)
            if mid:
                mid()
            low(u + SLOTS, B_UNITS, B_UNITS // 2)
            combine(G, columns, u, s, dst)

        def row_group(u, mid=None, mid_at=4):
            n = min(A_UNITS, UNITS - (u + SLOTS))
            low(u + SLOTS, mid_at)
            if mid:
                mid()
            low(u + SLOTS, n, mid_at)

        def turned(n, X, g0):
            dve.wait_ge(tr_hi, n + 1)
            for k in range(2):
                kt = 2 * (n % STEPS) + k
                last = V_.scalar_tensor_tensor(X[:, kt, 256:512], ps[:, 4 + n % 4, 256 * k:256 * (k + 1)],
                                               gT[:, g0 + kt:g0 + kt + 1], X[:, kt, 0:256].bitcast(f32),
                                               MULT, SUB)
            last.then_inc(tr_lo, 1)

        def rsqrt(st, dst, total, count):
            w = dst.shape[1]
            v, t, i = rs_v[:, 0:w], rs_t[:, 0:w], rs_i[:, 0:w].bitcast(i32)
            st.need()
            st.did(V_.tensor_scalar(v, total, 1.0 / count, RMS_EPS, MULT, ADD))
            st.need()
            st.did(V_.tensor_scalar(i, v.bitcast(i32), 1, None, ALU.logical_shift_right))
            st.need()
            st.did(V_.tensor_scalar(dst.bitcast(i32), i, -1.0, float(0x5f3759df), MULT, ADD))
            for _ in range(3):
                st.need()
                st.did(V_.tensor_tensor(t, dst, dst, MULT))
                st.need()
                st.did(V_.scalar_tensor_tensor(t, t, -0.5, v, MULT, MULT))
                st.need()
                st.did(V_.scalar_tensor_tensor(dst, t, 1.5, dst, ADD, MULT))

        def square_sums(st, src, junk, dst):
            for t in range(TT):
                st.need()
                st.did(V_.tensor_tensor_reduce(junk, src[:, t, :], src[:, t, :], 1.0, 0.0, MULT, ADD,
                                               dst[:, t:t + 1]))

        def split_branch(st, src, k):
            hi_v, lo_v = XC[:, k, 0:SEQ], XC[:, k, SEQ:]
            st.need()
            st.did(V_.tensor_scalar(hi_v, src, 1.0, None, MULT))
            st.need()
            V_.tensor_tensor(lo_v, src, hi_v.bitcast(f32), SUB).then_inc(branch_ready, 1)

        st = Steps(dve, dve_step)
        dve.wait_ge(norm_turned, 1)
        V_.tensor_copy(gT, ps[:, 7, 0:64]).then_inc(norm_ready, 1)
        dve.wait_ge(norm_ready, 1)
        for n in range(STEPS):
            turned(N_MEM0 + n, XB, 2 * KT)
            if n < SLOTS:
                low(0, n + 1, n)
        for i in range(4):
            dve.wait_ge(mem_loaded[i], 16)
        square_sums(st, mem_raw, gpost, ss[:, 0:2])
        rsqrt(st, mem_rstd, ss[:, 0:2], D_MODEL)
        st.need()
        dve.wait_ge(const_ready, 3)
        for t in range(TT):
            V_.tensor_scalar(diag[:, P * t:P * (t + 1)], ident, mem_rstd[:, t:t + 1], None, MULT)\
              .then_inc(diag_ready, 1)
        row = mem_rstd_row.unsqueeze(1).broadcast_to([P, 2, MEM_LEN])

        def keys(G, columns, u, s, i, row_first=False):
            low(u + SLOTS, B_UNITS)
            if row_first:
                dve.wait_ge(row_done, 1)
                V_.tensor_copy(mem_rstd_row, ps[:, 7, 0:256]).then_inc(row_copied, 1)
                dve.wait_ge(row_copied, 1)
            combine(G, columns, u, s, kmT[:, 2 * i:2 * i + 2, :])
            dve.wait_ge(bank_free, G + 1)
            V_.tensor_tensor(kmT[:, 2 * i:2 * i + 2, :], kmT[:, 2 * i:2 * i + 2, :], row, MULT)\
              .then_inc(km_ready, 1)

        keys(G_KM0, 0, U_KM0, 0, 0, row_first=True)
        dve.wait_ge(x_loaded, 16)
        square_sums(st, xres, gpost, ss[:, 2:4])
        rsqrt(st, x_rstd, ss[:, 2:4], D_MODEL)
        st.need()
        V_.tensor_scalar(subg, x_rstd[:, 0:1], 0.0, None, MULT).then_inc(x_stat, 1)
        keys(G_KM0 + 1, 1, U_KM0 + B_UNITS, 1, 1)
        for n in range(4):
            turned(N_X + n, XA, 0)
        row_group(U_VM0, mid=lambda: [turned(N_X + n, XA, 0) for n in range(4, 8)])

        dve.wait_ge(misc_loaded, 16 * 5)
        ang, turns, neg = area[:, 0:256], area[:, 256:512], area[:, 512:768]

        def op(ins):
            st.did(ins)
            st.need()
        dve.wait_ge(x_stat, 1)
        op(V_.tensor_scalar(subg, subg_raw, 0.5 * (1.0 - LAMBDA_INIT), None, MULT))
        op(V_.tensor_copy(ang, pos_i))
        op(V_.tensor_scalar(ang, ang, inv_freq, None, MULT))
        op(V_.tensor_scalar(turns, ang, 1.0 / (2 * math.pi), ROUND, MULT, ADD))
        op(V_.tensor_scalar(turns, turns, ROUND, None, SUB))
        for part in TWO_PI:
            op(V_.scalar_tensor_tensor(ang, turns, -part, ang, MULT, ADD))
        op(V_.tensor_scalar(ang, ang, PI_BELOW, -PI_BELOW, MIN, MAX))
        op(V_.tensor_scalar(sinT, ang, rope_sign, None, MULT))
        op(V_.tensor_scalar(neg, ang, -1.0, None, MULT))
        op(V_.tensor_tensor(neg, ang, neg, MIN))
        op(V_.tensor_scalar(cosT, neg, 1.0, math.pi / 2, MULT, ADD))
        for i in range(2):
            st.did(V_.tensor_tensor_reduce(area[:, 768 + 64 * i:832 + 64 * i], lam_in[:, 128 * i:128 * i + 64],
                                           lam_in[:, 128 * i + 64:128 * i + 128], 1.0, 0.0, MULT, ADD,
                                           lam_dot[:, i:i + 1]))
        st.need()
        V_.memset(upad[:, :, 0:2], 0.0).then_inc(angle_ready, 1)

        column_group(G_QM0, 2, U_QM0, 1, qmT[:, 0:2, :])
        for n in range(4):
            turned(N_MEM1 + n, XB, 3 * KT)
        dve.wait_ge(table_ready, 1)
        op(V_.tensor_tensor(neg_lam, lam_exp[:, 1:2], lam_exp[:, 0:1], SUB))
        op(V_.tensor_scalar(neg_lam, neg_lam, LAMBDA_INIT, None, SUB))
        column_group(G_QM0 + 1, 3, U_QM0 + B_UNITS, 0, qmT[:, 2:4, :])
        for n in range(4, 8):
            turned(N_MEM1 + n, XB, 3 * KT)

        def silu_twice(tanhs, tanh, gate, dst):
            dve.wait_ge(tanh_done, tanhs)
            return V_.scalar_tensor_tensor(dst, tanh, 1.0, gate, ADD, MULT)

        def cross_max(l):
            dve.wait_ge(xs_done, l + 1)
            op(V_.tensor_reduce(xmax, ps[:, 4:8, :].rearrange("p h (t k) -> p (h t) k", t=2), AX, MAX))
            V_.tensor_scalar(xnegmax, xmax, -X_SCALE, None, MULT).then_inc(xmax_ready, 1)

        def cross_normalise(l):
            dve.wait_ge(xexp_done, 8 * (l + 1))
            op(V_.reciprocal(xrcp, xsum))
            for g in range(8):
                last = V_.tensor_scalar(xprob[l][:, g, :], xprob[l][:, g, :], xrcp[:, g:g + 1], None, MULT)
                if g < 7:
                    st.did(last)
            last.then_inc(xprob_ready, 1)

        column_group(G_XG0, 4, U_XG0, 1, val0)
        op(silu_twice(1, xin, val0, xgate[:, 0:2, :]))
        cross_max(0)
        cross_normalise(0)
        column_group(G_XG0 + 1, 5, U_XG0 + B_UNITS, 0, val0)
        op(silu_twice(2, xin, val0, xgate[:, 2:4, :]))

        before_mix, MIX_STEPS = st.n, 11
        with dve.Fori(0, PAIRS) as j:
            st = Steps(dve, dve_step, before_mix + j * MIX_STEPS)
            G, c, u = j * 4 + G_MIX, j * 4 + columns_before(G_MIX, 1), j * (4 * B_UNITS) + U_MIX

            def mixer_group(g, dst):
                column_group(G + g, c + g, u + B_UNITS * g, (G_MIX + g) % 2, dst)
                dve.wait_ge(bank_free, G + (g + 1))
            mixer_group(0, xin)
            mixer_group(1, val0)
            st.did(V_.tensor_tensor(upad[:, :, 2:], val0, xin, MULT))
            st.need()
            for i in range(CONV_WIDTH):
                for t in range(2):
                    tap = convw[:, bass.ds(j * (2 * CONV_WIDTH) + (CONV_WIDTH * t + i), 1)]
                    uk = upad[:, t, i:i + SEQ]
                    if i == 0:
                        st.did(V_.tensor_scalar(conv[:, t, :], uk, tap, None, MULT))
                    else:
                        st.did(V_.scalar_tensor_tensor(conv[:, t, :], uk, tap, conv[:, t, :], MULT, ADD))
                st.need()
            mixer_group(2, val0)
            st.did(V_.tensor_tensor(conv, conv, val0, MULT))
            mixer_group(3, val0)
            st.did(silu_twice(j + 3, xin, val0, val0))
            st.need()
            st.did(V_.scalar_tensor_tensor(val0, val0, 0.5, conv, MULT, MULT))
            split_branch(st, val0, bass.ds(j * 2, 2))
            assert st.n == MIX_STEPS, st.n
        st = Steps(dve, dve_step, before_mix + PAIRS * MIX_STEPS)

        def op(ins):
            st.did(ins)
            st.need()

        dve.wait_ge(xo_done, 1)
        cross_o = ps[:, 4:6, :].rearrange("p b (h t) -> p (b h) t", h=2)
        op(V_.scalar_tensor_tensor(xg_flat, ps[:, 4:6, :].rearrange("p b c -> p (b c)"), 0.5, xg_flat, MULT, MULT))
        split_branch(st, xgate, slice(12, 16))

        def out_group(l, g, G, u, **kw):
            row_group(u, **kw)
            dve.wait_ge(bank_free, G + 1)
            yg = y_all[:, :, ACOLS * g:ACOLS * (g + 1)]
            for t in range(TT):
                op(V_.tensor_tensor_reduce(y_junk, yg[:, t, :], yg[:, t, :], 1.0, 0.0, MULT, ADD,
                                           y_ss[:, 4 * t + g:4 * t + g + 1]))
            dve.wait_ge(gpost_loaded, 16 * (l + 1))
            gp = gpost[:, ACOLS * g:ACOLS * (g + 1)].unsqueeze(1).broadcast_to([P, TT, ACOLS])
            op(V_.tensor_tensor(yg, yg, gp, MULT))

        def y_norm():
            op(V_.tensor_reduce(ss[:, 0:2], y_ss.rearrange("p (t g) -> p t g", t=TT), AX, ADD))
            rsqrt(st, y_rstd, ss[:, 0:2], D_MODEL)
            st.need()

        dve.wait_ge(branch_ready, PAIRS + 1)
        for g in range(4):
            out_group(0, g, G_OUT0 + g, U_OUT0 + A_UNITS * g)
        y_norm()
        dve.wait_ge(x_loaded, 32)
        for t in range(TT):
            op(V_.scalar_tensor_tensor(xres[:, t, :], y_all[:, t, :], y_rstd[:, t:t + 1], xres[:, t, :], MULT, ADD))
        V_.memset(cols[:, 95:96], 0.0).then_inc(xo_taken, 1)
        keys(G_KM1, columns_before(G_KM1, 5), U_KM1, G_KM1 % 2, 0)
        square_sums(st, xres, y_all[:, 0, :], ss[:, 2:4])
        rsqrt(st, x_rstd, ss[:, 2:4], D_MODEL)
        st.need()
        V_.memset(cols[:, 95:96], 0.0).then_inc(x_stat, 1)
        keys(G_KM1 + 1, columns_before(G_KM1, 5) + 1, U_KM1 + B_UNITS, (G_KM1 + 1) % 2, 1)
        for n in range(4):
            turned(N_H1 + n, XA, KT)
        row_group(U_VM1, mid=lambda: [turned(N_H1 + n, XA, KT) for n in range(4, 8)])
        for i in range(2):
            column_group(G_QM1 + i, columns_before(G_QM1, 6) + i, U_QM1 + B_UNITS * i, (G_QM1 + i) % 2,
                         qmT[:, 2 * i:2 * i + 2, :])
        row_group(U_V)
        cross_max(1)
        cross_normalise(1)
        row_group(U_V + A_UNITS)
        row_group(U_V + 2 * A_UNITS)
        dve.wait_ge(xo_done, 2)
        V_.tensor_copy(crossT1, cross_o).then_inc(xo_taken, 1)

        cos2 = cosT.unsqueeze(1).broadcast_to([P, 2, SEQ])
        sin2 = sinT.unsqueeze(1).broadcast_to([P, 2, SEQ])
        mask4 = mask.unsqueeze(1).unsqueeze(1).broadcast_to([P, 2, 2, P])

        def two(ap):
            return ap.rearrange("p (c t) -> p c t", c=2)

        def rope(st, loads, t, rot):
            dve.wait_ge(rot_loaded, loads)
            st.did(V_.tensor_tensor(two(rot), two(rot), sin2, MULT))
            st.did(V_.tensor_tensor(two(t), two(t), cos2, MULT))
            st.need()
            V_.tensor_tensor(t, t, rot, ADD).then_inc(rope_done, 1)

        def out_norm(st, p):
            dve.wait_ge(o_copied, p + 1)
            st.did(V_.tensor_tensor(o_sq, o_sb, o_sb, MULT))
            st.need()
            st.did(V_.tensor_reduce(ss[:, 4:8], o_sq, AX, ADD))
            rsqrt(st, o_rstd, ss[:, 4:8], HEAD_DIM)
            st.need()
            V_.tensor_tensor(o_sb, o_sb, o_rstd.unsqueeze(2).broadcast_to([P, 4, P]), MULT)\
              .then_inc(on_ready, 1)

        def out_take(st, p, parity):
            dve.wait_ge(n_done, p + 1)
            st.did(V_.scalar_tensor_tensor(br1, two(ps[:, 7, :]), subg, sgate[parity], MULT, MULT))
            split_branch(st, br1, bass.ds(p * 2, 2))

        def softmax(st, p):
            dve.wait_ge(s_done, p + 1)
            for sc in (score0, score1[:, :, :, P:]):
                st.did(V_.tensor_tensor(sc, sc, mask4, ADD))
            st.need()
            mx = xmax.rearrange("p (m h t) -> p m h t", m=2, h=2)
            st.did(V_.tensor_reduce(mx[:, :, :, 0], score0, AX, MAX))
            st.did(V_.tensor_reduce(mx[:, :, :, 1], score1, AX, MAX))
            st.need()
            V_.tensor_scalar(xnegmax, xmax, -D_SCALE, None, MULT).then_inc(max_ready, 1)
            dve.wait_ge(exp_done, p * 8 + 8)
            st.did(V_.reciprocal(xrcp, xsum))
            st.need()
            st.did(V_.tensor_scalar(xrcp[:, 4:8], xrcp[:, 4:8], neg_lam, None, MULT))
            st.need()
            segs = [(h, t, slice(P * t, P * (1 + 2 * t))) for h in range(2) for t in range(TT)]
            for h, t, seg in segs:
                st.did(V_.tensor_scalar(prob[:, h, 0, seg], prob[:, h, 0, seg],
                                        xrcp[:, 2 * h + t:2 * h + t + 1], None, MULT))
            st.need()
            for h, t, seg in segs:
                last = V_.scalar_tensor_tensor(prob[:, h, 0, seg], prob[:, h, 1, seg],
                                               xrcp[:, 4 + 2 * h + t:5 + 2 * h + t], prob[:, h, 0, seg],
                                               MULT, ADD)
            last.then_inc(w_ready, 1)

        def pair(st, p, s, parity, first=False):
            G, c, u = p * 3 + G_PAIR, p * 3 + columns_before(G_PAIR, 9), p * (3 * B_UNITS) + U_PAIR

            def in_keys():
                rope(st, p * 128 + 64, qT, qrot)
                if not first:
                    out_norm(st, p - 1)

            def in_gate():
                rope(st, p * 128 + 128, kT, krot)
                if not first:
                    out_take(st, p - 1, 1 - parity)
            column_group(G, c, u, s, two(qT))
            column_group(G + 1, c + 1, u + B_UNITS, 1 - s, two(kT), mid=in_keys)
            column_group(G + 2, c + 2, u + 2 * B_UNITS, s, val1, mid=in_gate)
            dve.wait_ge(bank_free, G + 3)
            st.did(silu_twice(p + (PAIRS + 3), tanh1, val1, sgate[parity]))
            softmax(st, p)

        pair(st, 0, G_PAIR % 2, 0, first=True)
        before_pairs, TWO_PAIR_STEPS = st.base + st.n, 2 * (4 + 14 + 2 + 11)
        with dve.Fori(1, PAIRS - 1, 2) as p:
            st = Steps(dve, dve_step, before_pairs + (p - 1) * (TWO_PAIR_STEPS // 2))
            pair(st, p, (G_PAIR + 1) % 2, 1)
            pair(st, p + 1, G_PAIR % 2, 0)
            assert st.n == TWO_PAIR_STEPS, st.n
        st = Steps(dve, dve_step, before_pairs + (PAIRS - 2) * (TWO_PAIR_STEPS // 2))
        pair(st, PAIRS - 1, (G_PAIR + 1) % 2, 1)

        def cross_branch(i, tanhs):
            G = G_XG1 + i
            dve.wait_ge(bank_free, G + 1)
            op(silu_twice(tanhs, tanh1, val1, val1))
            op(V_.scalar_tensor_tensor(val1, val1, 0.5, crossT1[:, 2 * i:2 * i + 2, :], MULT, MULT))
            split_branch(st, val1, slice(12 + 2 * i, 14 + 2 * i))

        columns = columns_before(G_XG1, 9)
        column_group(G_XG1, columns, U_XG1, G_XG1 % 2, val1)
        cross_branch(0, 2 * PAIRS + 3)
        column_group(G_XG1 + 1, columns + 1, U_XG1 + B_UNITS, (G_XG1 + 1) % 2, val1,
                     mid=lambda: out_norm(st, PAIRS - 1))
        cross_branch(1, 2 * PAIRS + 4)
        out_group(1, 0, G_OUT1, U_OUT1, mid=lambda: out_take(st, PAIRS - 1, 1), mid_at=2)
        for g in range(1, 4):
            out_group(1, g, G_OUT1 + g, U_OUT1 + A_UNITS * g, mid_at=2)
        y_norm()
        for t in range(TT):
            for h in range(2):
                part = slice(1024 * h, 1024 * (h + 1))
                V_.scalar_tensor_tensor(xres[:, t, part], y_all[:, t, part], y_rstd[:, t:t + 1],
                                        xres[:, t, part], MULT, ADD).then_inc(out_ready, 1)

    block_cm.__exit__(None, None, None)


_INS = ['x', 'mem', 'positions', 'pre_norm', 'post_norm', 'mem_norm', 'w_in', 'w_kv_mem', 'w_out',
        'conv_w', 'diff_lambda', 'diff_subln']


def kernel(**inputs):
    import concourse.bacc as _bacc
    from concourse.bass_utils import run_bass_kernel_spmd as _run

    nc = _bacc.Bacc("TRN2", target_bir_lowering=False, num_devices=1)
    arrays, args = {}, []

    def give(name, a):
        arrays[f"in_{name}_dram"] = a
        args.append(nc.dram_tensor(f"in_{name}_dram", a.shape, mybir.dt.from_np(a.dtype),
                                   kind="ExternalInput").ap())
    for name in _INS:
        give(name, np.ascontiguousarray(inputs[name]))
    d = np.arange(P) % (DIFF_DIM // 2)
    freq = np.float32(ROPE_THETA) ** (-(2 * d).astype(np.float32) / np.float32(DIFF_DIM))
    sign = np.where(np.arange(P) % DIFF_DIM < DIFF_DIM // 2, -1.0, 1.0)
    give("rope_consts", np.stack([freq, sign], axis=1).astype(np.float32))
    args.append(nc.dram_tensor("out_0_dram", (1, SEQ, D_MODEL), mybir.dt.float32,
                               kind="ExternalOutput").ap())
    build(nc, *args)
    r = _run(nc, [arrays], core_ids=[0])
    return r.results[0]["out_0_dram"]
```

```python
import math

import numpy as np
import concourse.bass as bass
from concourse import mybir

D_MODEL, SEQ, MEM_LEN, DEPTH = 2048, 256, 256, 2
HEAD_DIM, CROSS_HEADS, DIFF_DIM, CONV_WIDTH = 128, 4, 64, 3
CROSS_WIDTH = CROSS_HEADS * HEAD_DIM
TOK_WIDTH = D_MODEL - CROSS_WIDTH
ROPE_THETA, RMS_EPS, NEG_BIG = 10000.0, 1e-6, -1e30

P = 128
KT = D_MODEL // P
TT = SEQ // P
BCOLS = 256
ACOLS = 512
UNIT = 1024
SLOTS = 4
B_UNITS = KT * BCOLS // UNIT
A_UNITS = KT * ACOLS // UNIT
B_KT = KT // B_UNITS
A_KT = KT // A_UNITS
PAIRS = TOK_WIDTH // BCOLS
QM_COL = 3 * TOK_WIDTH
GATE_COL = QM_COL + CROSS_WIDTH
XGATE_COL = GATE_COL + TOK_WIDTH
OUT_ORDER = [0, 2, 4, 6, 8, 12, 14, 10]
STORES = [(0, 0, 1024), (0, 1024, 2048)] + [(1, ACOLS * g, ACOLS * (g + 1)) for g in range(4)]
LAMBDA_INIT = 0.8 - 0.6 * math.exp(-0.3 * 1)
TWO_PI = (6.28125, 2029 / 2 ** 20, 2 * math.pi - 6.28125 - 2029 / 2 ** 20)
ROUND = 1.5 * 2.0 ** 23
PI_BELOW = 3.1415925

G_KM0, U_KM0 = 0, 0
G_VM0, U_VM0 = 2, 8
G_QM0, U_QM0 = 3, 16
G_XG0, U_XG0 = 5, 24
G_MIX, U_MIX = 7, 32
G_OUT0, U_OUT0 = 31, 128
G_KM1, U_KM1 = 35, 160
G_VM1, U_VM1 = 37, 168
G_QM1, U_QM1 = 38, 176
G_V, U_V = 40, 184
G_PAIR, U_PAIR = 43, 208
G_XG1, U_XG1 = 61, 280
G_OUT1, U_OUT1 = 63, 288
UNITS = U_OUT1 + 4 * A_UNITS

STEPS = KT // 2
N_MEM0, N_X, N_MEM1, N_H1 = 0, STEPS, 2 * STEPS, 3 * STEPS


def columns_before(G, row_groups):
    return G - row_groups


class Steps:

    def __init__(self, eng, sem, base=0):
        self.eng, self.sem, self.base, self.n = eng, sem, base, 0

    def did(self, ins):
        ins.then_inc(self.sem, 1)
        self.n += 1

    def need(self):
        if isinstance(self.base, int) and self.base + self.n == 0:
            return
        self.eng.wait_ge(self.sem, self.base + self.n)


def build(nc, x_in, mem_in, positions, pre_norm, post_norm, mem_norm, w_in, w_kv_mem, w_out,
          conv_w, diff_lambda, diff_subln, rope_consts, out):
    f32, f32r, i32 = mybir.dt.float32, mybir.dt.float32r, mybir.dt.int32
    ALU, ACT, AX = mybir.AluOpType, mybir.ActivationFunctionType, mybir.AxisListType.X

    def sb(name, shape, dt=f32):
        return nc.alloc_sbuf_tensor(name, shape, dt).ap()

    XA = sb("hT_split", [P, KT, 2 * SEQ], f32r)
    XC = sb("branchT_split", [P, KT, 2 * SEQ], f32r)
    xb_at = -(-nc.sbuf_base // 32) * 32
    XB = sb("memT_split", [P, KT, 2 * MEM_LEN], f32r)
    L1 = nc.alloc_sbuf_tensor_at("layer1_area", [P, KT * 2 * MEM_LEN], f32, offset=xb_at).ap()
    xres = sb("x_residual", [P, TT, D_MODEL])
    S = sb("stage_area", [P, 2 * D_MODEL])
    raw = sb("raw_ring", [P, SLOTS, UNIT])
    whi = sb("hi_ring", [P, SLOTS, UNIT], f32r)
    wlo = sb("lo_ring", [P, SLOTS, UNIT], f32r)
    kmT = sb("kmT", [P, CROSS_HEADS, MEM_LEN])
    vm = sb("vm", [P, MEM_LEN // P, CROSS_WIDTH])
    qmT = sb("qmT", [P, CROSS_HEADS, SEQ])
    area = sb("layer0_area", [P, D_MODEL + 4])
    small = sb("small_terms", [P, 2, 256])
    xgate = sb("cross_gate0", [P, CROSS_HEADS, SEQ])
    ident = sb("ident", [P, P])
    mask = sb("causal_mask", [P, P])
    cosT = sb("cosT", [P, SEQ])
    sinT = sb("sinT", [P, SEQ])
    mem_rstd_row = sb("mem_rstd_row", [P, MEM_LEN])
    gT = sb("normT", [P, 2 * DEPTH * KT])
    convw = sb("convw", [P, 2 * PAIRS * CONV_WIDTH])
    cols = sb("columns", [P, 96])

    mem_raw = S.rearrange("p (t d) -> p t d", t=TT)
    y_all = S.rearrange("p (t d) -> p t d", t=TT)
    V = S[:, 0:TT * TOK_WIDTH].rearrange("p (t d) -> p t d", t=TT)
    tanh1 = S[:, 3072:3584].rearrange("p (c t) -> p c t", c=2)
    br1 = S[:, 3584:4096].rearrange("p (c t) -> p c t", c=2)
    xprob = [a[:, 0:2048].rearrange("p (h k) -> p h k", h=2 * CROSS_HEADS) for a in (S, L1)]
    xprobT = [a[:, 2048:4096].rearrange("p (h k) -> p h k", h=CROSS_HEADS) for a in (S, L1)]
    crossT1 = L1[:, 7168:8192].rearrange("p (h t) -> p h t", h=CROSS_HEADS)

    def l1(at):
        return L1[:, at:at + 512]
    qT, qrot, kT, krot = l1(0), l1(512), l1(1024), l1(1536)
    sgate = [l1(2048).rearrange("p (c t) -> p c t", c=2), l1(2560).rearrange("p (c t) -> p c t", c=2)]
    prob = L1[:, 3072:4608].rearrange("p (h m k) -> p h m k", h=2, m=2)
    probT = L1[:, 4608:5376].rearrange("p (h k) -> p h k", h=2)
    o_sb = l1(5376).rearrange("p (g e) -> p g e", g=4)
    o_sq = l1(5888).rearrange("p (g e) -> p g e", g=4)
    val1 = l1(6400).rearrange("p (c t) -> p c t", c=2)
    gpost = area[:, 0:D_MODEL]
    xin = area[:, 0:512].rearrange("p (c t) -> p c t", c=2)
    val0 = area[:, 512:1024].rearrange("p (c t) -> p c t", c=2)
    conv = area[:, 1024:1536].rearrange("p (c t) -> p c t", c=2)
    upad = area[:, 1536:2052].rearrange("p (c t) -> p c t", c=2)
    xg_flat = xgate.rearrange("p h t -> p (h t)")
    norm_rows = xg_flat[0:64, 0:128]
    diag, ones = xg_flat[:, 640:896], xg_flat[:, 896:1024]
    y_junk = [xg_flat[:, 0:512], xg_flat[:, 512:1024]]
    q_of_map = [xg_flat[:, 0:512], xg_flat[:, 512:1024]]
    pos_i, lam_in = S[:, 3072:3328].bitcast(i32), S[:, 3328:3584]
    turns, neg = S[:, 3584:3840], S[:, 3840:4096]
    inv_freq, rope_sign, subg = cols[:, 0:1], cols[:, 1:2], cols[:, 2:3]
    mem_rstd, x_rstd, y_rstd = cols[:, 4:6], cols[:, 6:8], cols[:, 8:10]
    lam_dot, lam_exp, neg_lam = cols[:, 10:12], cols[:, 12:14], cols[:, 14:15]
    ss = cols[:, 16:24]
    y_ss = cols[:, 24:32]
    rs_v, rs_t, rs_i = cols[:, 32:36], cols[:, 36:40], cols[:, 40:44]
    xmax, xnegmax, xsum, xrcp = (cols[:, 44 + 8 * i:52 + 8 * i] for i in range(4))
    o_rstd = cols[:, 76:80]
    subg_raw, o_eps = cols[:, 80:81], cols[:, 82:86]

    ps = nc.alloc_psum_tensor("psum", [P, 8, 512], f32).ap()

    def banks(s):
        return ps[:, 2 * s:2 * s + 2, :]

    score = ps[:, 4:8, :].rearrange("p (m b) c -> p m b c", b=2)
    score1 = score[:, :, 0, :].rearrange("p m (h k) -> p m h k", h=2)
    score0 = score[:, :, 1, 0:256].rearrange("p m (h k) -> p m h k", h=2)

    def sem(name):
        return nc.alloc_semaphore(name)

    raw_loaded = [sem(f"raw_loaded{i}") for i in range(SLOTS)]
    hi_ready, lo_ready = sem("hi_ready"), sem("lo_ready")
    unit_done, half_done = sem("unit_done"), sem("half_done")
    small_copied = sem("small_copied")
    bank_free = sem("bank_free")
    mem_loaded = [sem(f"mem_loaded{i}") for i in range(4)]
    x_loaded, rows_loaded, misc_loaded = sem("x_loaded"), sem("rows_loaded"), sem("misc_loaded")
    gpost_loaded, rot_loaded, out_stored = sem("gpost_loaded"), sem("rot_loaded"), sem("out_stored")
    late_loaded = sem("positions_lambda_loaded")
    mem_squared, x_squared, x_new = sem("mem_squared"), sem("x_squared"), sem("x_new")
    y_squared, y_taken = sem("y_squared"), sem("y_taken")
    ident_step, const_ready = sem("ident_step"), sem("const_ready")
    tr_done, tr_hi, tr_lo = sem("tr_done"), sem("tr_hi"), sem("tr_lo")
    norm_turned, norm_ready = sem("norm_turned"), sem("norm_ready")
    diag_ready, row_done, row_copied = sem("diag_ready"), sem("row_done"), sem("row_copied")
    xs_ready = sem("xs_ready")
    angle_ready, table_ready = sem("angle_ready"), sem("table_ready")
    km_ready = sem("km_ready")
    xs_done, xmax_ready, xexp_done, xprob_ready = (sem("xscore_done"), sem("xmax_ready"),
                                                   sem("xexp_done"), sem("xprob_ready"))
    xt_done, xpt_ready, xo_done, xo_taken = sem("xturn_done"), sem("xprobT_ready"), sem("xout_done"), sem("xout_taken")
    tanh_done, branch_ready = sem("tanh_done"), sem("branch_ready")
    rope_done, s_done, max_ready, exp_done = sem("rope_done"), sem("score_done"), sem("max_ready"), sem("exp_done")
    w_ready, wt_done, wt_ready = sem("weights_ready"), sem("weights_turned"), sem("weightsT_ready")
    pv_done, o_copied, on_ready, n_done, o_taken = sem("pv_done"), sem("o_copied"), sem("o_normed"), sem("o_turned"), sem("o_taken")
    out_ready = sem("out_ready")
    dve_step = sem("dve_step")

    X_SCALE, D_SCALE = HEAD_DIM ** -0.5, DIFF_DIM ** -0.5
    block_cm = nc.Block()
    block = block_cm.__enter__()

    @block.sync
    def _(sp):
        def unit(u, slot, dst, src):
            if not isinstance(u, int) or u >= SLOTS:
                sp.wait_ge(lo_ready, u - SLOTS + 1)
            sp.dma_start(dst, src).then_inc(raw_loaded[slot], 16)

        def column_group(u, w, col, at={}):
            w = w.rearrange("(k p) n -> p k n", p=P)
            for n in range(B_UNITS):
                if n in at:
                    at[n]()
                unit(u + n, n % SLOTS, raw[:, n % SLOTS, :].rearrange("p (k c) -> p k c", k=B_KT),
                     w[:, B_KT * n:B_KT * (n + 1), bass.ds(col, BCOLS)])

        def row_group(u, w, col, order):
            w = w.rearrange("(k p) n -> p k n", p=P)
            for n, k in enumerate(order):
                unit(u + n, n % SLOTS, raw[:, n % SLOTS, :].rearrange("p (k c) -> p k c", k=A_KT),
                     w[:, k:k + A_KT, col:col + ACOLS])

        in_order = list(range(0, KT, A_KT))
        mem_v = mem_in[0].rearrange("(t p) d -> p t d", p=P)

        def load_mem(i):
            sp.dma_start(mem_raw[:, :, 512 * i:512 * (i + 1)], mem_v[:, :, 512 * i:512 * (i + 1)])\
              .then_inc(mem_loaded[i], 16)

        def load_rest():
            sp.dma_start(xres, x_in[0].rearrange("(t p) d -> p t d", p=P)).then_inc(x_loaded, 16)
            sp.dma_start(cols[:, 0:2], rope_consts).then_inc(misc_loaded, 16)
            sp.dma_start(subg_raw, diff_subln[0].rearrange("(p a) -> p a", a=1)).then_inc(misc_loaded, 16)
            sp.dma_start(convw.rearrange("p (t k) -> p t k", k=CONV_WIDTH),
                         conv_w[0].rearrange("(t p) k -> p t k", p=P)).then_inc(misc_loaded, 16)

        first_loads = {i: lambda i=i: load_mem(i) for i in range(4)}
        other_loads = {1: load_rest}

        def memory(l, u):
            for i in range(2):
                column_group(u + B_UNITS * i, w_kv_mem[l], BCOLS * i, at=first_loads if l + i == 0 else
                             other_loads if l == 0 else {})
            row_group(u + 2 * B_UNITS, w_kv_mem[l], CROSS_WIDTH, in_order)

        memory(0, U_KM0)
        for i in range(2):
            column_group(U_QM0 + B_UNITS * i, w_in[0], QM_COL + BCOLS * i)
        for i in range(2):
            column_group(U_XG0 + B_UNITS * i, w_in[0], XGATE_COL + BCOLS * i)
        with sp.Fori(0, PAIRS) as j:
            for g, col in enumerate((0, 2 * TOK_WIDTH, TOK_WIDTH, GATE_COL)):
                column_group(j * (4 * B_UNITS) + (U_MIX + B_UNITS * g), w_in[0], j * BCOLS + col)
        for g in range(4):
            row_group(U_OUT0 + A_UNITS * g, w_out[0], ACOLS * g, OUT_ORDER)
        memory(1, U_KM1)
        for i in range(2):
            column_group(U_QM1 + B_UNITS * i, w_in[1], QM_COL + BCOLS * i)
        for g in range(3):
            row_group(U_V + A_UNITS * g, w_in[1], 2 * TOK_WIDTH + ACOLS * g, in_order)

        def swap_halves(G, src, dst):
            sp.wait_ge(bank_free, G + 1)
            for b in range(4):
                o = 32 * (b ^ 1)
                sp.dma_start(dst[32 * b:32 * b + 32, :], src[o:o + 32, :]).then_inc(rot_loaded, 16)

        def pair(p, first=False):
            for g, col in enumerate((0, TOK_WIDTH, GATE_COL)):
                column_group(p * (3 * B_UNITS) + (U_PAIR + B_UNITS * g), w_in[1], p * BCOLS + col)
                if g == 0 and not first:
                    swap_halves(p * 3 + (G_PAIR - 2), kT, krot)
            swap_halves(p * 3 + G_PAIR, qT, qrot)

        pair(0, first=True)
        with sp.Fori(1, PAIRS) as p:
            pair(p)
        column_group(U_XG1, w_in[1], XGATE_COL)
        swap_halves(G_PAIR + 3 * PAIRS - 2, kT, krot)
        column_group(U_XG1 + B_UNITS, w_in[1], XGATE_COL + BCOLS)
        for g in range(4):
            row_group(U_OUT1 + A_UNITS * g, w_out[1], ACOLS * g, OUT_ORDER)
        for n, (t, lo_col, hi_col) in enumerate(STORES):
            sp.wait_ge(out_ready, n + 1)
            sp.dma_start(out[0, P * t:P * (t + 1), lo_col:hi_col], xres[:, t, lo_col:hi_col]).then_inc(out_stored, 16)
        sp.wait_ge(out_stored, 16 * len(STORES))

    @block.gpsimd
    def _(pool):
        nc.gpsimd.memset(ident, 0.0).then_inc(ident_step, 1)
        nc.gpsimd.memset(mask, 0.0).then_inc(ident_step, 1)
        nc.gpsimd.memset(ones, 1.0).then_inc(const_ready, 1)
        pool.wait_ge(ident_step, 2)
        nc.gpsimd.affine_select(out=ident, in_=ident, compare_op=ALU.not_equal, fill=1.0, base=0,
                                pattern=[[-1, P]], channel_multiplier=1).then_inc(const_ready, 1)
        nc.gpsimd.affine_select(out=mask, in_=mask, compare_op=ALU.is_ge, fill=NEG_BIG, base=0,
                                pattern=[[-1, P]], channel_multiplier=1).then_inc(const_ready, 1)

    @block.tensor
    def _(pe):
        mm = nc.tensor.matmul

        def first_bank_wait(G):
            if not isinstance(G, int) or G >= 2:
                pe.wait_ge(bank_free, G - 1)

        def column_group(G, u, s, X, x_steps=None, at={}):
            first_bank_wait(G)
            for n in range(B_UNITS):
                if n in at:
                    at[n]()
                if x_steps is not None:
                    pe.wait_ge(tr_lo, x_steps + 2 * (n + 1))
                pe.wait_ge(lo_ready, u + n + 1)
                hi = whi[:, n % SLOTS, :].rearrange("p (k c) -> p k c", k=B_KT)
                lo = wlo[:, n % SLOTS, :].rearrange("p (k c) -> p k c", k=B_KT)
                for k in range(B_KT):
                    kt = B_KT * n + k
                    for c in range(2):
                        o = banks(s)[:, c, :]
                        mm(o, hi[:, k, P * c:P * (c + 1)], X[:, kt, :], start=kt == 0, stop=False)
                        last = mm(o[:, SEQ:], lo[:, k, P * c:P * (c + 1)], X[:, kt, 0:SEQ],
                                  start=False, stop=kt == KT - 1)
                last.then_inc(unit_done, 1)

        def row_group(G, u, s, X, order, before=None, at={}, half_first=False):
            first_bank_wait(G)
            steps = [(n, (0, 1)) for n in range(A_UNITS)]
            if half_first:
                steps = steps[:-SLOTS] + [(n, (t,)) for t in range(TT) for n in range(A_UNITS - SLOTS, A_UNITS)]
            for n, tiles in steps:
                if 0 in tiles:
                    if n in at:
                        at[n]()
                    if before:
                        before(n)
                    pe.wait_ge(lo_ready, u + n + 1)
                hi = whi[:, n % SLOTS, :].rearrange("p (k c) -> p k c", k=A_KT)
                lo = wlo[:, n % SLOTS, :].rearrange("p (k c) -> p k c", k=A_KT)
                for k in range(A_KT):
                    for t in tiles:
                        k0 = order[n]
                        xh = X[:, k0 + k, P * t:P * (t + 1)]
                        xl = X[:, k0 + k, SEQ + P * t:SEQ + P * (t + 1)]
                        o = banks(s)[:, t, :]
                        first, final = n == 0 and k == 0, n == len(order) - 1 and k == A_KT - 1
                        mm(o, xl, hi[:, k, :], start=first, stop=False)
                        mm(o, xh, lo[:, k, :], start=False, stop=False)
                        last = mm(o, xh, hi[:, k, :], start=False, stop=final)
                if 1 in tiles:
                    last.then_inc(unit_done, 1)
                elif n == A_UNITS - 1:
                    last.then_inc(half_done, 1)

        def turn(n, src, ready=None):
            if n >= 4:
                pe.wait_ge(tr_lo, n - 3)
            if ready:
                ready()
            for k in range(2):
                kt = 2 * (n % STEPS) + k
                for t in range(TT):
                    last = nc.tensor.transpose(ps[:, 4 + n % 4, 256 * k + P * t:256 * k + P * (t + 1)],
                                               src[:, t, P * kt:P * (kt + 1)], ident)
            last.then_inc(tr_done, 1)

        def cross_scores(l):
            pe.wait_ge(km_ready, l + 1)
            for h in range(CROSS_HEADS):
                for t in range(TT):
                    last = mm(ps[:, 4 + h, 256 * t:256 * (t + 1)], qmT[:, h, P * t:P * (t + 1)],
                              kmT[:, h, :], start=True, stop=True)
            last.then_inc(xs_done, 1)

        def cross_turn(l):
            pe.wait_ge(xprob_ready, l + 1)
            for h in range(CROSS_HEADS):
                for m in range(MEM_LEN // P):
                    for t in range(TT):
                        last = nc.tensor.transpose(ps[:, 4 + h, 256 * m + P * t:256 * m + P * (t + 1)],
                                                   xprob[l][:, 2 * h + t, P * m:P * (m + 1)], ident)
                last.then_inc(xt_done, 1)

        def cross_values(l):
            pe.wait_ge(xpt_ready, 4 * (l + 1))
            for h in range(CROSS_HEADS):
                for m in range(MEM_LEN // P):
                    last = mm(ps[:, 4 + h // 2, 256 * (h % 2):256 * (h % 2) + 256],
                              vm[:, m, P * h:P * (h + 1)], xprobT[l][:, h, 256 * m:256 * (m + 1)],
                              start=m == 0, stop=m == 1)
            last.then_inc(xo_done, 1)

        in_order = list(range(0, KT, A_KT))

        pe.wait_ge(const_ready, 3)
        pe.wait_ge(rows_loaded, 32)
        nc.tensor.transpose(ps[:, 7, 0:64], norm_rows, ident[0:64, 0:64]).then_inc(norm_turned, 1)

        def mem_turns(*steps):
            for n in steps:
                if n % 2 == 0:
                    pe.wait_ge(mem_loaded[n // 2], 16)
                if n == 3:
                    pe.wait_ge(norm_ready, 1)
                turn(N_MEM0 + n, mem_raw)

        def turns_of(first, steps, src, ready=None):
            def run():
                if ready:
                    ready()
                for n in steps:
                    turn(first + n, src)
            return run

        mem_turns(0, 1, 2, 3)
        column_group(G_KM0, U_KM0, 0, XB, x_steps=N_MEM0,
                     at={1: lambda: mem_turns(4, 5), 2: lambda: mem_turns(6, 7)})
        column_group(G_KM0 + 1, U_KM0 + B_UNITS, 1, XB)
        pe.wait_ge(diag_ready, 2)
        pe.wait_ge(tr_lo, STEPS)
        for t in range(TT):
            last = mm(ps[:, 7, P * t:P * (t + 1)], ones, diag[:, P * t:P * (t + 1)], start=True, stop=True)
        last.then_inc(row_done, 1)

        def x_ready():
            pe.wait_ge(xs_ready, 2)
            pe.wait_ge(row_copied, 1)
        row_group(G_VM0, U_VM0, 0, XB, in_order,
                  at={4: turns_of(N_X, range(4), xres, x_ready), 6: turns_of(N_X, range(4, 8), xres)})
        column_group(G_QM0, U_QM0, 1, XA, x_steps=N_X)
        for n in range(4):
            turn(N_MEM1 + n, mem_raw)
        column_group(G_QM0 + 1, U_QM0 + B_UNITS, 0, XA)
        for n in range(4, 8):
            turn(N_MEM1 + n, mem_raw)
        column_group(G_XG0, U_XG0, 1, XA)
        pe.wait_ge(bank_free, G_QM0 + 2)
        pe.wait_ge(tr_lo, N_MEM1 + STEPS)
        cross_scores(0)
        column_group(G_XG0 + 1, U_XG0 + B_UNITS, 0, XA)
        cross_turn(0)
        with pe.Fori(0, PAIRS) as j:
            for g in range(4):
                column_group(j * 4 + (G_MIX + g), j * (4 * B_UNITS) + (U_MIX + B_UNITS * g),
                             (G_MIX + g) % 2, XA)
        pe.wait_ge(bank_free, G_VM0 + 1)
        cross_values(0)

        def y_wait(i):
            pe.wait_ge(y_squared, 2 * i + 2)

        def branch_wait(counts):
            def before(n):
                if n in counts:
                    pe.wait_ge(branch_ready, counts[n])
            return before

        for g in range(4):
            if g >= 2:
                y_wait(g - 2)
            row_group(G_OUT0 + g, U_OUT0 + A_UNITS * g, (G_OUT0 + g) % 2, XC, OUT_ORDER,
                      before=branch_wait({0: PAIRS - 1, 5: PAIRS + 1}))
        y_wait(2)
        column_group(G_KM1, U_KM1, G_KM1 % 2, XB, x_steps=N_MEM1)
        y_wait(3)
        column_group(G_KM1 + 1, U_KM1 + B_UNITS, (G_KM1 + 1) % 2, XB)
        row_group(G_VM1, U_VM1, G_VM1 % 2, XB, in_order,
                  at={1: turns_of(N_H1, range(4), y_all, lambda: pe.wait_ge(xs_ready, 4)),
                      4: turns_of(N_H1, range(4, 8), y_all)})
        column_group(G_QM1, U_QM1, G_QM1 % 2, XA, x_steps=N_H1)
        column_group(G_QM1 + 1, U_QM1 + B_UNITS, (G_QM1 + 1) % 2, XA)
        for g in range(3):
            row_group(G_V + g, U_V + A_UNITS * g, (G_V + g) % 2, XA, in_order)
            if g == 0:
                pe.wait_ge(bank_free, G_QM1 + 2)
                cross_scores(1)
            elif g == 1:
                cross_turn(1)
            else:
                cross_values(1)

        def diff_turn(p):
            pe.wait_ge(w_ready, p + 1)
            for h in range(2):
                for b in range(3):
                    last = nc.tensor.transpose(ps[:, 4 + h, P * b:P * (b + 1)],
                                               prob[:, h, 0, P * b:P * (b + 1)], ident)
            last.then_inc(wt_done, 1)

        def diff_values(p):
            pe.wait_ge(wt_ready, p + 1)
            for h in range(2):
                o = ps[:, 6, 256 * h:256 * (h + 1)]
                v = [V[:, t, bass.ds(p * (2 * P) + P * h, P)] for t in range(TT)]
                mm(o[:, 0:P], probT[:, h, 0:P], v[0], start=True, stop=True)
                mm(o[:, P:], probT[:, h, P:2 * P], v[0], start=True, stop=False)
                last = mm(o[:, P:], probT[:, h, 2 * P:], v[1], start=False, stop=True)
            last.then_inc(pv_done, 1)

        def diff_out_turn(p):
            pe.wait_ge(on_ready, p + 1)
            for g in range(4):
                last = nc.tensor.transpose(ps[:, 7, P * g:P * (g + 1)], o_sb[:, g, :], ident)
            last.then_inc(n_done, 1)

        def diff_scores(p, first=False):
            pe.wait_ge(rope_done, p * 2 + 2)
            if not first:
                pe.wait_ge(o_taken, p)
            for m in range(2):
                for h in range(2):
                    for t in range(TT):
                        o = (score0 if t == 0 else score1)[:, m, h, :]
                        last = mm(o, q_of_map[m][:, 256 * h + P * t:256 * h + P * (t + 1)],
                                  kT[:, 256 * h:256 * h + P * (t + 1)], start=True, stop=True)
            last.then_inc(s_done, 1)

        def pair(p, s, first=False, second=False):
            G, u = p * 3 + G_PAIR, p * (3 * B_UNITS) + U_PAIR
            column_group(G, u, s, XA, at={} if first else {1: lambda: diff_scores(p - 1, second)})
            column_group(G + 1, u + B_UNITS, 1 - s, XA,
                         at={} if first else {2: lambda: diff_turn(p - 1), 3: lambda: diff_values(p - 1)})
            column_group(G + 2, u + 2 * B_UNITS, s, XA, at={} if first else {3: lambda: diff_out_turn(p - 1)})

        pair(0, G_PAIR % 2, first=True)
        pe.wait_ge(xo_taken, 1)
        pair(1, (G_PAIR + 1) % 2, second=True)
        with pe.Fori(2, PAIRS, 2) as p:
            pair(p, G_PAIR % 2)
            pair(p + 1, (G_PAIR + 1) % 2)
        column_group(G_XG1, U_XG1, G_XG1 % 2, XA, at={1: lambda: diff_scores(PAIRS - 1)})
        column_group(G_XG1 + 1, U_XG1 + B_UNITS, (G_XG1 + 1) % 2, XA,
                     at={2: lambda: diff_turn(PAIRS - 1), 3: lambda: diff_values(PAIRS - 1)})
        done0 = PAIRS + 1
        for g in range(4):
            if g >= 2:
                y_wait(4 + g - 2)
            row_group(G_OUT1 + g, U_OUT1 + A_UNITS * g, (G_OUT1 + g) % 2, XC, OUT_ORDER,
                      before=branch_wait({0: done0 + PAIRS - 1, 5: done0 + PAIRS, 6: done0 + PAIRS + 1,
                                          7: done0 + PAIRS + 2}),
                      at={4: lambda: diff_out_turn(PAIRS - 1)} if g == 0 else {},
                      half_first=g == 3)

    @block.scalar
    def _(act):
        run = nc.scalar.activation
        act.dma_start(norm_rows[0:32, :], pre_norm.rearrange("l (k p) -> (l k) p", p=P)).then_inc(rows_loaded, 16)
        act.dma_start(norm_rows[32:64, :], mem_norm.rearrange("l (k p) -> (l k) p", p=P)).then_inc(rows_loaded, 16)
        act.wait_ge(const_ready, 1)
        run(cols[:, 94:95], ones[:, 0:1], ACT.Copy)

        def high(u, n, n0=0):
            for i in range(n0, n):
                slot = i % SLOTS
                act.wait_ge(raw_loaded[slot], (u + (i - slot)) * (16 // SLOTS) + 16)
                if not isinstance(u, int) or u + i >= SLOTS:
                    act.wait_ge(unit_done, u + (i - SLOTS + 1))
                run(whi[:, slot, :], raw[:, slot, :], ACT.Copy).then_inc(hi_ready, 1)

        def take_small(G, u, s):
            act.wait_ge(unit_done, u + B_UNITS)
            if not isinstance(G, int) or G >= 1:
                act.wait_ge(bank_free, G)
            run(small, banks(s)[:, :, SEQ:], ACT.Copy).then_inc(small_copied, 1)

        def ahead(u, n, at):
            for i in range(n):
                if i in at:
                    at[i]()
                high(u + SLOTS, i + 1, i)

        def column_group(G, u, s, at={}):
            ahead(u, B_UNITS, at)
            take_small(G, u, s)

        def row_group(G, u, s, outs, scale=None, at={}):
            ahead(u, A_UNITS, at)
            act.wait_ge(unit_done, u + A_UNITS)
            act.wait_ge(bank_free, G)
            if scale is None:
                run(outs, banks(s), ACT.Copy).then_inc(bank_free, 1)
            else:
                run(outs[:, 0, :], banks(s)[:, 0, :], ACT.Copy, scale=scale[:, 0:1])
                run(outs[:, 1, :], banks(s)[:, 1, :], ACT.Copy, scale=scale[:, 1:2]).then_inc(bank_free, 1)

        def out_group(i, u, s, at={}):
            ahead(u, min(A_UNITS, UNITS - (u + SLOTS)), at)
            for t in range(TT):
                if i == 2 * 4 - 1 and t == 0:
                    act.wait_ge(half_done, 1)
                else:
                    act.wait_ge(unit_done, u + A_UNITS)
                if t == 1:
                    act.wait_ge(y_taken, i + 1)
                if i > 0:
                    act.wait_ge(y_squared, 2 * i + t - 1)
                c = 4 * t + i % 4
                run(y_junk[t], banks(s)[:, t, :], ACT.Square, accum_out=y_ss[:, c:c + 1])\
                    .then_inc(y_squared, 1)

        def squares(src, junk, dst, done):
            run(junk, src, ACT.Square, accum_out=dst).then_inc(done, 1)

        def turned(n, X, g0):
            act.wait_ge(tr_done, n + 1)
            for k in range(2):
                kt = 2 * (n % STEPS) + k
                last = run(X[:, kt, 0:256], ps[:, 4 + n % 4, 256 * k:256 * (k + 1)], ACT.Copy,
                           scale=gT[:, g0 + kt:g0 + kt + 1])
            last.then_inc(tr_hi, 1)

        def cross_exp(l):
            act.wait_ge(xmax_ready, l + 1)
            for g in range(2 * CROSS_HEADS):
                run(xprob[l][:, g, :], ps[:, 4 + g // 2, 256 * (g % 2):256 * (g % 2) + 256], ACT.Exp,
                    bias=xnegmax[:, g:g + 1], scale=X_SCALE, accum_out=xsum[:, g:g + 1]).then_inc(xexp_done, 1)

        def cross_take(l):
            for h in range(CROSS_HEADS):
                act.wait_ge(xt_done, 4 * l + h + 1)
                run(xprobT[l][:, h, :], ps[:, 4 + h, :], ACT.Copy).then_inc(xpt_ready, 1)

        def steps_of(first, steps, X, g0):
            return lambda: [turned(first + n, X, g0) for n in steps]

        act.wait_ge(norm_ready, 1)
        for n in range(STEPS):
            turned(N_MEM0 + n, XB, 2 * KT)
            if n % 2:
                high(0, n // 2 + 1, n // 2)
        column_group(G_KM0, U_KM0, 0)
        for t in range(TT):
            if t == 1:
                act.wait_ge(mem_squared, 1)
            for i in range(4):
                act.wait_ge(mem_loaded[i], 16)
            squares(mem_raw[:, t, :], gpost, ss[:, t:t + 1], mem_squared)
        column_group(G_KM0 + 1, U_KM0 + B_UNITS, 1)
        act.wait_ge(x_loaded, 16)
        for t in range(TT):
            act.wait_ge(*((x_squared, 1) if t else (mem_squared, 2)))
            squares(xres[:, t, :], gpost, ss[:, 2 + t:3 + t], x_squared)
        row_group(G_VM0, U_VM0, 0, vm, scale=mem_rstd,
                  at={4: steps_of(N_X, range(4), XA, 0), 6: steps_of(N_X, range(4, 8), XA, 0)})
        act.wait_ge(tr_lo, N_X + STEPS)
        act.dma_start(xres, x_in[0].rearrange("(t p) d -> p t d", p=P)).then_inc(x_loaded, 16)
        column_group(G_QM0, U_QM0, 1)
        for n in range(4):
            turned(N_MEM1 + n, XB, 3 * KT)
        column_group(G_QM0 + 1, U_QM0 + B_UNITS, 0)
        for n in range(4, 8):
            turned(N_MEM1 + n, XB, 3 * KT)

        def tanh_of(G, src, dst):
            act.wait_ge(bank_free, G + 1)
            run(dst, src, ACT.Tanh, scale=0.5).then_inc(tanh_done, 1)

        column_group(G_XG0, U_XG0, 1)
        tanh_of(G_XG0, val0, xin)
        cross_exp(0)
        column_group(G_XG0 + 1, U_XG0 + B_UNITS, 0)
        tanh_of(G_XG0 + 1, val0, xin)
        cross_take(0)
        with act.Fori(0, PAIRS) as j:
            for g in range(4):
                G = j * 4 + (G_MIX + g)
                column_group(G, j * (4 * B_UNITS) + (U_MIX + B_UNITS * g), (G_MIX + g) % 2)
            tanh_of(G, val0, xin)
        act.wait_ge(branch_ready, PAIRS + 1)
        act.dma_start(gpost, post_norm[0:1, :].partition_broadcast(P)[:, 0, :]).then_inc(gpost_loaded, 16)
        for g in range(4):
            out_group(g, U_OUT0 + A_UNITS * g, (G_OUT0 + g) % 2)
        column_group(G_KM1, U_KM1, G_KM1 % 2)
        for t in range(TT):
            act.wait_ge(x_new, t + 1)
            squares(xres[:, t, :], y_all[:, t, :], ss[:, 2 + t:3 + t], x_squared)
        act.dma_start(gpost, post_norm[1:2, :].partition_broadcast(P)[:, 0, :]).then_inc(gpost_loaded, 16)
        column_group(G_KM1 + 1, U_KM1 + B_UNITS, (G_KM1 + 1) % 2)
        row_group(G_VM1, U_VM1, G_VM1 % 2, vm, scale=mem_rstd,
                  at={1: steps_of(N_H1, range(4), XA, KT), 4: steps_of(N_H1, range(4, 8), XA, KT)})
        act.wait_ge(tr_lo, N_H1 + STEPS)
        act.dma_start(pos_i, positions[0:1, :].partition_broadcast(P)[:, 0, :]).then_inc(late_loaded, 16)
        act.dma_start(lam_in, diff_lambda.rearrange("l a d -> l (a d)").partition_broadcast(P)[:, 0, :])\
           .then_inc(late_loaded, 16)
        column_group(G_QM1, U_QM1, G_QM1 % 2)
        column_group(G_QM1 + 1, U_QM1 + B_UNITS, (G_QM1 + 1) % 2)
        def tables():
            act.wait_ge(angle_ready, 1)
            run(cosT, cosT, ACT.Sin)
            run(sinT, sinT, ACT.Sin)
            run(lam_exp, lam_dot, ACT.Exp).then_inc(table_ready, 1)

        for g in range(3):
            row_group(G_V + g, U_V + A_UNITS * g, (G_V + g) % 2, V[:, :, ACOLS * g:ACOLS * (g + 1)],
                      at={2: tables} if g == 2 else {})
            if g == 0:
                cross_exp(1)
            elif g == 1:
                cross_take(1)

        def take_weights(p):
            act.wait_ge(wt_done, p + 1)
            run(probT, ps[:, 4:6, 0:3 * P], ACT.Copy).then_inc(wt_ready, 1)

        def take_values(p):
            act.wait_ge(pv_done, p + 1)
            o = ps[:, 6, :].rearrange("p (g e) -> p g e", g=4)
            run(o_sb, o, ACT.Copy).then_inc(o_copied, 1)
            for g in range(4):
                run(o_sq[:, g, :], o[:, g, :], ACT.Square, accum_out=ss[:, 4 + g:5 + g]).then_inc(o_copied, 1)

        def exps(p):
            act.wait_ge(max_ready, p + 1)
            for m in range(2):
                for h in range(2):
                    for t in range(TT):
                        i = 4 * m + 2 * h + t
                        run(prob[:, h, m, P * t:P * (1 + 2 * t)], (score0 if t == 0 else score1)[:, m, h, :],
                            ACT.Exp, bias=xnegmax[:, i:i + 1], scale=D_SCALE,
                            accum_out=xsum[:, i:i + 1]).then_inc(exp_done, 1)

        def pair(p, s, first=False):
            G, u = p * 3 + G_PAIR, p * (3 * B_UNITS) + U_PAIR
            column_group(G, u, s, at={} if first else {2: lambda: exps(p - 1)})
            column_group(G + 1, u + B_UNITS, 1 - s,
                         at={} if first else {2: lambda: take_weights(p - 1), 3: lambda: take_values(p - 1)})
            column_group(G + 2, u + 2 * B_UNITS, s)
            tanh_of(G + 2, val1, tanh1)

        pair(0, G_PAIR % 2, first=True)
        with act.Fori(1, PAIRS - 1, 2) as p:
            pair(p, (G_PAIR + 1) % 2)
            pair(p + 1, G_PAIR % 2)
        pair(PAIRS - 1, (G_PAIR + 1) % 2)
        column_group(G_XG1, U_XG1, G_XG1 % 2, at={2: lambda: exps(PAIRS - 1)})
        tanh_of(G_XG1, val1, tanh1)
        column_group(G_XG1 + 1, U_XG1 + B_UNITS, (G_XG1 + 1) % 2,
                     at={2: lambda: take_weights(PAIRS - 1), 3: lambda: take_values(PAIRS - 1)})
        tanh_of(G_XG1 + 1, val1, tanh1)
        for g in range(4):
            out_group(4 + g, U_OUT1 + A_UNITS * g, (G_OUT1 + g) % 2)

    @block.vector
    def _(dve):
        V_ = nc.vector
        MULT, ADD, SUB, MAX, MIN = ALU.mult, ALU.add, ALU.subtract, ALU.max, ALU.min

        def low(u, n, n0=0):
            for i in range(n0, n):
                slot = i % SLOTS
                dve.wait_ge(hi_ready, u + (i + 1))
                V_.tensor_tensor(wlo[:, slot, :], raw[:, slot, :], whi[:, slot, :].bitcast(f32), SUB)\
                  .then_inc(lo_ready, 1)

        def combine(G, columns, u, s, dst):
            dve.wait_ge(lo_ready, u + (SLOTS + B_UNITS))
            dve.wait_ge(small_copied, columns + 1)
            V_.tensor_tensor(dst, banks(s)[:, :, 0:SEQ], small, ADD).then_inc(bank_free, 1)

        def ahead(u, n, at):
            for i in range(n):
                if i in at:
                    at[i]()
                low(u + SLOTS, i + 1, i)

        def column_group(G, columns, u, s, dst, at={}):
            ahead(u, B_UNITS, at)
            combine(G, columns, u, s, dst)

        def row_group(u, at={}):
            ahead(u, min(A_UNITS, UNITS - (u + SLOTS)), at)

        def turned(n, X, g0):
            dve.wait_ge(tr_hi, n + 1)
            for k in range(2):
                kt = 2 * (n % STEPS) + k
                last = V_.scalar_tensor_tensor(X[:, kt, 256:512], ps[:, 4 + n % 4, 256 * k:256 * (k + 1)],
                                               gT[:, g0 + kt:g0 + kt + 1], X[:, kt, 0:256].bitcast(f32),
                                               MULT, SUB)
            last.then_inc(tr_lo, 1)

        def rsqrt(st, dst, total, count, eps=None):
            w = dst.shape[1]
            v, t, i = rs_v[:, 0:w], rs_t[:, 0:w], rs_i[:, 0:w].bitcast(i32)
            st.need()
            if eps is None:
                st.did(V_.tensor_scalar(v, total, 1.0 / count, RMS_EPS, MULT, ADD))
            else:
                st.did(V_.scalar_tensor_tensor(v, total, 1.0 / count, eps, MULT, ADD))
            st.need()
            st.did(V_.tensor_scalar(i, v.bitcast(i32), 1, None, ALU.logical_shift_right))
            st.need()
            st.did(V_.tensor_scalar(dst.bitcast(i32), i, -1.0, float(0x5f3759df), MULT, ADD))
            for _ in range(3):
                st.need()
                st.did(V_.tensor_tensor(t, dst, dst, MULT))
                st.need()
                st.did(V_.scalar_tensor_tensor(t, t, -0.5, v, MULT, MULT))
                st.need()
                st.did(V_.scalar_tensor_tensor(dst, t, 1.5, dst, ADD, MULT))

        def split_branch(st, src, k):
            hi_v, lo_v = XC[:, k, 0:SEQ], XC[:, k, SEQ:]
            st.need()
            st.did(V_.tensor_scalar(hi_v, src, 1.0, None, MULT))
            st.need()
            V_.tensor_tensor(lo_v, src, hi_v.bitcast(f32), SUB).then_inc(branch_ready, 1)

        st = Steps(dve, dve_step)
        dve.wait_ge(norm_turned, 1)
        V_.tensor_copy(gT, ps[:, 7, 0:64]).then_inc(norm_ready, 1)
        dve.wait_ge(norm_ready, 1)

        def steps_of(first, steps, X, g0):
            return lambda: [turned(first + n, X, g0) for n in steps]

        def op(ins):
            st.did(ins)
            st.need()

        for n in range(STEPS):
            turned(N_MEM0 + n, XB, 2 * KT)
            if n % 2:
                low(0, n // 2 + 1, n // 2)
        column_group(G_KM0, 0, U_KM0, 0, kmT[:, 0:2, :])

        def mem_stat():
            dve.wait_ge(mem_squared, 2)
            rsqrt(st, mem_rstd, ss[:, 0:2], D_MODEL)
            st.need()
            dve.wait_ge(const_ready, 3)
            for t in range(TT):
                V_.tensor_scalar(diag[:, P * t:P * (t + 1)], ident, mem_rstd[:, t:t + 1], None, MULT)\
                  .then_inc(diag_ready, 1)
        column_group(G_KM0 + 1, 1, U_KM0 + B_UNITS, 1, kmT[:, 2:4, :], at={0: mem_stat})
        row = mem_rstd_row.unsqueeze(1).broadcast_to([P, CROSS_HEADS, MEM_LEN])

        def scale_keys(l):
            dve.wait_ge(bank_free, (G_KM0, G_KM1)[l] + 2)
            V_.tensor_tensor(kmT, kmT, row, MULT).then_inc(km_ready, 1)

        def take_row():
            dve.wait_ge(row_done, 1)
            V_.tensor_copy(mem_rstd_row, ps[:, 7, 0:256]).then_inc(row_copied, 1)
            dve.wait_ge(row_copied, 1)
            scale_keys(0)

        def scale_x(count, dst):
            dve.wait_ge(x_squared, count)
            rsqrt(st, x_rstd, ss[:, 2:4], D_MODEL)
            st.need()
            for t in range(TT):
                V_.tensor_scalar(dst[:, t, :], xres[:, t, :], x_rstd[:, t:t + 1], None, MULT).then_inc(xs_ready, 1)

        row_group(U_VM0, at={0: take_row, 1: lambda: scale_x(2, xres), 4: steps_of(N_X, range(4), XA, 0),
                             6: steps_of(N_X, range(4, 8), XA, 0)})
        column_group(G_QM0, 2, U_QM0, 1, qmT[:, 0:2, :])
        for n in range(4):
            turned(N_MEM1 + n, XB, 3 * KT)
        column_group(G_QM0 + 1, 3, U_QM0 + B_UNITS, 0, qmT[:, 2:4, :])
        for n in range(4, 8):
            turned(N_MEM1 + n, XB, 3 * KT)
        dve.wait_ge(misc_loaded, 16 * 3)
        op(V_.memset(upad[:, :, 0:2], 0.0))
        op(V_.tensor_scalar(subg, subg_raw, 0.5 * (1.0 - LAMBDA_INIT), None, MULT))

        def silu_twice(tanhs, tanh, gate, dst):
            dve.wait_ge(tanh_done, tanhs)
            return V_.scalar_tensor_tensor(dst, tanh, 1.0, gate, ADD, MULT)

        def cross_max(l):
            dve.wait_ge(xs_done, l + 1)
            op(V_.tensor_reduce(xmax, ps[:, 4:8, :].rearrange("p h (t k) -> p (h t) k", t=2), AX, MAX))
            V_.tensor_scalar(xnegmax, xmax, -X_SCALE, None, MULT).then_inc(xmax_ready, 1)

        def cross_normalise(l):
            dve.wait_ge(xexp_done, 8 * (l + 1))
            op(V_.reciprocal(xrcp, xsum))
            for g in range(8):
                last = V_.tensor_scalar(xprob[l][:, g, :], xprob[l][:, g, :], xrcp[:, g:g + 1], None, MULT)
                if g < 7:
                    st.did(last)
            last.then_inc(xprob_ready, 1)

        column_group(G_XG0, 4, U_XG0, 1, val0)
        op(silu_twice(1, xin, val0, xgate[:, 0:2, :]))
        cross_max(0)
        cross_normalise(0)
        column_group(G_XG0 + 1, 5, U_XG0 + B_UNITS, 0, val0)
        op(silu_twice(2, xin, val0, xgate[:, 2:4, :]))

        before_mix, MIX_STEPS = st.n, 11
        with dve.Fori(0, PAIRS) as j:
            st = Steps(dve, dve_step, before_mix + j * MIX_STEPS)
            G, c, u = j * 4 + G_MIX, j * 4 + columns_before(G_MIX, 1), j * (4 * B_UNITS) + U_MIX

            def mixer_group(g, dst):
                column_group(G + g, c + g, u + B_UNITS * g, (G_MIX + g) % 2, dst)
                dve.wait_ge(bank_free, G + (g + 1))
            mixer_group(0, xin)
            mixer_group(1, val0)
            st.did(V_.tensor_tensor(upad[:, :, 2:], val0, xin, MULT))
            st.need()
            for i in range(CONV_WIDTH):
                for t in range(2):
                    tap = convw[:, bass.ds(j * (2 * CONV_WIDTH) + (CONV_WIDTH * t + i), 1)]
                    uk = upad[:, t, i:i + SEQ]
                    if i == 0:
                        st.did(V_.tensor_scalar(conv[:, t, :], uk, tap, None, MULT))
                    else:
                        st.did(V_.scalar_tensor_tensor(conv[:, t, :], uk, tap, conv[:, t, :], MULT, ADD))
                st.need()
            mixer_group(2, val0)
            st.did(V_.tensor_tensor(conv, conv, val0, MULT))
            mixer_group(3, val0)
            st.did(silu_twice(j + 3, xin, val0, val0))
            st.need()
            st.did(V_.scalar_tensor_tensor(val0, val0, 0.5, conv, MULT, MULT))
            split_branch(st, val0, bass.ds(j * 2, 2))
            assert st.n == MIX_STEPS, st.n
        st = Steps(dve, dve_step, before_mix + PAIRS * MIX_STEPS)

        dve.wait_ge(xo_done, 1)
        cross_o = ps[:, 4:6, :].rearrange("p b (h t) -> p (b h) t", h=2)
        op(V_.scalar_tensor_tensor(xg_flat, ps[:, 4:6, :].rearrange("p b c -> p (b c)"), 0.5, xg_flat, MULT, MULT))
        split_branch(st, xgate, slice(12, 16))

        def out_group(i, u, s, at={}):
            row_group(u, at)
            g, l = i % 4, i // 4
            dve.wait_ge(unit_done, u + A_UNITS)
            dve.wait_ge(gpost_loaded, 16 * (l + 1))
            part = slice(ACOLS * g, ACOLS * (g + 1))
            V_.tensor_tensor(y_all[:, 1, part], banks(s)[:, 1, :], gpost[:, part], MULT).then_inc(y_taken, 1)
            dve.wait_ge(y_squared, 2 * i + 1)
            V_.tensor_tensor(y_all[:, 0, part], banks(s)[:, 0, :], gpost[:, part], MULT).then_inc(bank_free, 1)

        def y_norm(tiles):
            op(V_.tensor_reduce(ss[:, tiles], y_ss.rearrange("p (t g) -> p t g", t=TT)[:, tiles, :], AX, ADD))
            rsqrt(st, y_rstd[:, tiles], ss[:, tiles], D_MODEL)
            st.need()

        for g in range(4):
            out_group(g, U_OUT0 + A_UNITS * g, (G_OUT0 + g) % 2)
        dve.wait_ge(y_squared, 8)
        dve.wait_ge(bank_free, G_OUT0 + 4)
        y_norm(slice(0, 2))
        dve.wait_ge(x_loaded, 32)

        def add_y(t):
            V_.scalar_tensor_tensor(xres[:, t, :], y_all[:, t, :], y_rstd[:, t:t + 1], xres[:, t, :], MULT, ADD)\
              .then_inc(x_new, 1)
        column_group(G_KM1, columns_before(G_KM1, 5), U_KM1, G_KM1 % 2, kmT[:, 0:2, :],
                     at={1: lambda: add_y(0), 2: lambda: add_y(1)})
        column_group(G_KM1 + 1, columns_before(G_KM1, 5) + 1, U_KM1 + B_UNITS, (G_KM1 + 1) % 2, kmT[:, 2:4, :],
                     at={2: lambda: scale_x(4, y_all)})
        scale_keys(1)
        row_group(U_VM1, at={1: steps_of(N_H1, range(4), XA, KT), 4: steps_of(N_H1, range(4, 8), XA, KT)})
        for m in range(2):
            other = slice(DIFF_DIM * (1 - m), DIFF_DIM * (2 - m))
            st.did(V_.memset(q_of_map[m][other, :], 0.0))
        for i in range(2):
            column_group(G_QM1 + i, columns_before(G_QM1, 6) + i, U_QM1 + B_UNITS * i, (G_QM1 + i) % 2,
                         qmT[:, 2 * i:2 * i + 2, :])
        row_group(U_V)
        cross_max(1)
        cross_normalise(1)
        def angles():
            dve.wait_ge(late_loaded, 16 * 2)
            op(V_.tensor_copy(sinT, pos_i))
            op(V_.tensor_scalar(sinT, sinT, inv_freq, None, MULT))
            op(V_.tensor_scalar(turns, sinT, 1.0 / (2 * math.pi), ROUND, MULT, ADD))
            op(V_.tensor_scalar(turns, turns, ROUND, None, SUB))
            for part in TWO_PI:
                op(V_.scalar_tensor_tensor(sinT, turns, -part, sinT, MULT, ADD))
            op(V_.tensor_scalar(sinT, sinT, PI_BELOW, -PI_BELOW, MIN, MAX))
            op(V_.tensor_scalar(neg, sinT, -1.0, None, MULT))
            op(V_.tensor_tensor(neg, sinT, neg, MIN))
            op(V_.tensor_scalar(sinT, sinT, rope_sign, None, MULT))
            op(V_.tensor_scalar(cosT, neg, 1.0, math.pi / 2, MULT, ADD))
            for i in range(2):
                st.did(V_.tensor_tensor_reduce(turns[:, 64 * i:64 * (i + 1)], lam_in[:, 128 * i:128 * i + 64],
                                               lam_in[:, 128 * i + 64:128 * i + 128], 1.0, 0.0, MULT, ADD,
                                               lam_dot[:, i:i + 1]))
            st.need()
            V_.memset(cols[:, 95:96], 0.0).then_inc(angle_ready, 1)
        row_group(U_V + A_UNITS, at={4: angles})
        row_group(U_V + 2 * A_UNITS)
        dve.wait_ge(table_ready, 1)
        op(V_.tensor_tensor(neg_lam, lam_exp[:, 1:2], lam_exp[:, 0:1], SUB))
        op(V_.tensor_scalar(neg_lam, neg_lam, LAMBDA_INIT, None, SUB))
        dve.wait_ge(xo_done, 2)
        V_.tensor_copy(crossT1, cross_o).then_inc(xo_taken, 1)

        cos2 = cosT.unsqueeze(1).broadcast_to([P, 2, SEQ])
        sin2 = sinT.unsqueeze(1).broadcast_to([P, 2, SEQ])
        mask4 = mask.unsqueeze(1).unsqueeze(1).broadcast_to([P, 2, 2, P])

        def two(ap):
            return ap.rearrange("p (c t) -> p c t", c=2)

        def rope(st, loads, t, rot, dsts):
            dve.wait_ge(rot_loaded, loads)
            st.did(V_.tensor_tensor(two(rot), two(rot), sin2, MULT))
            st.did(V_.tensor_tensor(two(t), two(t), cos2, MULT))
            st.need()
            for rows, dst in dsts:
                last = V_.tensor_tensor(dst[rows, :], t[rows, :], rot[rows, :], ADD)
            last.then_inc(rope_done, 1)

        def out_norm(st, p):
            dve.wait_ge(o_copied, p * 5 + 5)
            rsqrt(st, o_rstd, ss[:, 4:8], HEAD_DIM, o_eps)
            st.need()
            V_.tensor_tensor(o_sb, o_sb, o_rstd.unsqueeze(2).broadcast_to([P, 4, P]), MULT)\
              .then_inc(on_ready, 1)

        def out_take(st, p, parity):
            dve.wait_ge(n_done, p + 1)
            V_.scalar_tensor_tensor(br1, two(ps[:, 7, :]), subg, sgate[parity], MULT, MULT).then_inc(o_taken, 1)
            dve.wait_ge(o_taken, p + 1)
            split_branch(st, br1, bass.ds(p * 2, 2))

        def softmax_max(st, p):
            dve.wait_ge(s_done, p + 1)
            for sc in (score0, score1[:, :, :, P:]):
                st.did(V_.tensor_tensor(sc, sc, mask4, ADD))
            st.need()
            mx = xmax.rearrange("p (m h t) -> p m h t", m=2, h=2)
            st.did(V_.tensor_reduce(mx[:, :, :, 0], score0, AX, MAX))
            st.did(V_.tensor_reduce(mx[:, :, :, 1], score1, AX, MAX))
            st.need()
            V_.tensor_scalar(xnegmax, xmax, -D_SCALE, None, MULT).then_inc(max_ready, 1)

        def softmax_weights(st, p):
            dve.wait_ge(exp_done, p * 8 + 8)
            sum0, rcp1 = xsum[:, 0:4], xrcp[:, 4:8]
            st.did(V_.reciprocal(rcp1, xsum[:, 4:8]))
            st.did(V_.scalar_tensor_tensor(o_eps, sum0, RMS_EPS, sum0, MULT, MULT))
            st.need()
            st.did(V_.scalar_tensor_tensor(rcp1, rcp1, neg_lam, sum0, MULT, MULT))
            st.need()
            for h in range(2):
                for t in range(TT):
                    seg = slice(P * t, P * (1 + 2 * t))
                    last = V_.scalar_tensor_tensor(prob[:, h, 0, seg], prob[:, h, 1, seg],
                                                   rcp1[:, 2 * h + t:2 * h + t + 1], prob[:, h, 0, seg],
                                                   MULT, ADD)
            last.then_inc(w_ready, 1)

        def pair(st, p, s, parity, first=False):
            G, c, u = p * 3 + G_PAIR, p * 3 + columns_before(G_PAIR, 9), p * (3 * B_UNITS) + U_PAIR

            def rope_keys():
                rope(st, p * 128 + 128, kT, krot, [(slice(0, P), kT)])
            in_query, in_keys, in_gate = {}, {}, {2: rope_keys}
            if not first:
                in_query = {1: lambda: softmax_max(st, p - 1), 2: lambda: softmax_weights(st, p - 1)}
                in_gate = {0: lambda: out_norm(st, p - 1), 2: rope_keys, 3: lambda: out_take(st, p - 1, 1 - parity)}
            in_keys[2] = lambda: rope(st, p * 128 + 64, qT, qrot,
                                      [(slice(64 * m, 64 * (m + 1)), q_of_map[m]) for m in range(2)])
            column_group(G, c, u, s, two(qT), at=in_query)
            column_group(G + 1, c + 1, u + B_UNITS, 1 - s, two(kT), at=in_keys)
            column_group(G + 2, c + 2, u + 2 * B_UNITS, s, val1, at=in_gate)
            dve.wait_ge(bank_free, G + 3)
            st.did(silu_twice(p + (PAIRS + 3), tanh1, val1, sgate[parity]))

        pair(st, 0, G_PAIR % 2, 0, first=True)
        before_pairs, TWO_PAIR_STEPS = st.base + st.n, 2 * (4 + 12 + 1 + 8)
        with dve.Fori(1, PAIRS - 1, 2) as p:
            st = Steps(dve, dve_step, before_pairs + (p - 1) * (TWO_PAIR_STEPS // 2))
            pair(st, p, (G_PAIR + 1) % 2, 1)
            pair(st, p + 1, G_PAIR % 2, 0)
            assert st.n == TWO_PAIR_STEPS, st.n
        st = Steps(dve, dve_step, before_pairs + (PAIRS - 2) * (TWO_PAIR_STEPS // 2))
        pair(st, PAIRS - 1, (G_PAIR + 1) % 2, 1)

        def cross_branch(i, tanhs):
            G = G_XG1 + i
            dve.wait_ge(bank_free, G + 1)
            op(silu_twice(tanhs, tanh1, val1, val1))
            op(V_.scalar_tensor_tensor(val1, val1, 0.5, crossT1[:, 2 * i:2 * i + 2, :], MULT, MULT))
            split_branch(st, val1, slice(12 + 2 * i, 14 + 2 * i))

        columns = columns_before(G_XG1, 9)
        column_group(G_XG1, columns, U_XG1, G_XG1 % 2, val1,
                     at={1: lambda: softmax_max(st, PAIRS - 1), 2: lambda: softmax_weights(st, PAIRS - 1)})
        cross_branch(0, 2 * PAIRS + 3)
        column_group(G_XG1 + 1, columns + 1, U_XG1 + B_UNITS, (G_XG1 + 1) % 2, val1)
        cross_branch(1, 2 * PAIRS + 4)
        for g in range(3):
            out_group(4 + g, U_OUT1 + A_UNITS * g, (G_OUT1 + g) % 2,
                      at={0: lambda: out_norm(st, PAIRS - 1), 4: lambda: out_take(st, PAIRS - 1, 1)}
                      if g == 0 else {})
        row_group(U_OUT1 + 3 * A_UNITS)
        part, last_banks = slice(3 * ACOLS, 4 * ACOLS), banks((G_OUT1 + 3) % 2)

        def finish(t, lo_col, hi_col):
            cols_ = slice(lo_col, hi_col)
            V_.scalar_tensor_tensor(xres[:, t, cols_], y_all[:, t, cols_], y_rstd[:, t:t + 1],
                                    xres[:, t, cols_], MULT, ADD).then_inc(out_ready, 1)
        dve.wait_ge(bank_free, G_OUT1 + 3)
        dve.wait_ge(y_squared, 15)
        op(V_.tensor_tensor(y_all[:, 0, part], last_banks[:, 0, :], gpost[:, part], MULT))
        y_norm(slice(0, 1))
        finish(0, *STORES[0][1:])
        dve.wait_ge(unit_done, UNITS)
        V_.tensor_tensor(y_all[:, 1, part], last_banks[:, 1, :], gpost[:, part], MULT).then_inc(y_taken, 1)
        finish(0, *STORES[1][1:])
        dve.wait_ge(y_taken, 8)
        dve.wait_ge(y_squared, 16)
        y_norm(slice(1, 2))
        for store in STORES[2:]:
            finish(*store)

    block_cm.__exit__(None, None, None)


_INS = ['x', 'mem', 'positions', 'pre_norm', 'post_norm', 'mem_norm', 'w_in', 'w_kv_mem', 'w_out',
        'conv_w', 'diff_lambda', 'diff_subln']


def kernel(**inputs):
    import concourse.bacc as _bacc
    from concourse.bass_utils import run_bass_kernel_spmd as _run

    nc = _bacc.Bacc("TRN2", target_bir_lowering=False, num_devices=1)
    arrays, args = {}, []

    def give(name, a):
        arrays[f"in_{name}_dram"] = a
        args.append(nc.dram_tensor(f"in_{name}_dram", a.shape, mybir.dt.from_np(a.dtype),
                                   kind="ExternalInput").ap())
    for name in _INS:
        give(name, np.ascontiguousarray(inputs[name]))
    d = np.arange(P) % (DIFF_DIM // 2)
    freq = np.float32(ROPE_THETA) ** (-(2 * d).astype(np.float32) / np.float32(DIFF_DIM))
    sign = np.where(np.arange(P) % DIFF_DIM < DIFF_DIM // 2, -1.0, 1.0)
    give("rope_consts", np.stack([freq, sign], axis=1).astype(np.float32))
    args.append(nc.dram_tensor("out_0_dram", (1, SEQ, D_MODEL), mybir.dt.float32,
                               kind="ExternalOutput").ap())
    build(nc, *args)
    r = _run(nc, [arrays], core_ids=[0])
    return r.results[0]["out_0_dram"]
```
